# Optimizing a Trainium2 kernel written in Bass

```python
import jax
import jax.numpy as jnp
from jax import lax
import numpy as np

D_MODEL = 1024
BATCH = 1
SEQ = 1024
DEPTH = 2

N_EVEN = (DEPTH + 1) // 2
N_ODD = DEPTH // 2

HEAD_DIM = 64
ATTN_HEADS = D_MODEL // (2 * HEAD_DIM)
ATTN_KV_HEADS = max(1, ATTN_HEADS // 4)
WINDOW = 128
ATTN_BLOCK = 128

SSM_D_INNER = D_MODEL // 2
SSM_HEAD_DIM = 64
SSM_HEADS = SSM_D_INNER // SSM_HEAD_DIM
SSM_GROUPS = 2
SSM_D_STATE = 128
SSM_CONV = 4
SSM_CHUNK = 128
SSM_CONV_CH = SSM_D_INNER + 2 * SSM_GROUPS * SSM_D_STATE

Q_COLS = ATTN_HEADS * HEAD_DIM
KV_COLS = ATTN_KV_HEADS * HEAD_DIM
MIX_WIDTH = Q_COLS + SSM_D_INNER
IN_COLS = Q_COLS + 2 * KV_COLS + SSM_D_INNER + SSM_CONV_CH + SSM_HEADS

CONV_CH = D_MODEL
CONV_KERNEL = 31

MOE_GROUPS = 4
MOE_EXPERTS_PER_GROUP = 8
MOE_EXPERTS = MOE_GROUPS * MOE_EXPERTS_PER_GROUP
MOE_TOP_K = 2
EXPERT_FF = D_MODEL // 2
MOE_BLOCK = 128

RMS_EPS = 1e-6
LN_EPS = 1e-5

kernel_name = 'hybrid_swa_ssd_conformer_hmoe'

def rms_norm(x, g):
    xf = x.astype(jnp.float32)
    y = xf * lax.rsqrt(jnp.mean(xf * xf, axis=-1, keepdims=True) + RMS_EPS)
    return (y * g.astype(jnp.float32)).astype(x.dtype)

def layer_norm(x, g, b):
    xf = x.astype(jnp.float32)
    mu = jnp.mean(xf, axis=-1, keepdims=True)
    var = jnp.mean(jnp.square(xf - mu), axis=-1, keepdims=True)
    y = (xf - mu) * lax.rsqrt(var + LN_EPS)
    return (y * g.astype(jnp.float32) + b.astype(jnp.float32)).astype(x.dtype)

def causal_depthwise_conv(x, w, b):
    k_width, ch = w.shape
    y = lax.conv_general_dilated(
        x, w[:, None, :].astype(x.dtype), window_strides=(1,), padding=[(k_width - 1, 0)],
        dimension_numbers=('NWC', 'WIO', 'NWC'), feature_group_count=ch)
    return y + b.astype(x.dtype)

def sliding_window_sink_attention(q, k, v, sinks):
    bsz, seq, n_heads, dh = q.shape
    n_kv = k.shape[2]
    rep = n_heads // n_kv
    blk = ATTN_BLOCK
    nb = seq // blk
    qb = q.reshape(bsz, nb, blk, n_kv, rep, dh)
    kb = k.reshape(bsz, nb, blk, n_kv, dh)
    vb = v.reshape(bsz, nb, blk, n_kv, dh)
    pad = ((0, 0), (1, 0), (0, 0), (0, 0), (0, 0))
    kk = jnp.concatenate([jnp.pad(kb, pad)[:, :-1], kb], axis=2)
    vv = jnp.concatenate([jnp.pad(vb, pad)[:, :-1], vb], axis=2)
    s = jnp.einsum('bnqkgd,bnskd->bnkgqs', qb, kk).astype(jnp.float32) * (dh ** -0.5)
    qi = jnp.arange(blk)[:, None]
    kj = jnp.arange(2 * blk)[None, :]
    rel = qi + blk - kj
    band = (rel >= 0) & (rel < WINDOW)
    real_key = (jnp.arange(nb)[:, None, None] > 0) | (kj >= blk)[None]
    mask = band[None] & real_key
    s = jnp.where(mask[None, :, None, None], s, -jnp.inf)
    sink = sinks.astype(jnp.float32).reshape(n_kv, rep)[None, None, :, :, None, None]
    m = jnp.maximum(jnp.max(s, axis=-1, keepdims=True), sink)
    p = jnp.exp(s - m)
    denom = jnp.sum(p, axis=-1, keepdims=True) + jnp.exp(sink - m)
    probs = (p / denom).astype(v.dtype)
    o = jnp.einsum('bnkgqs,bnskd->bnqkgd', probs, vv)
    return o.reshape(bsz, seq, n_heads * dh)

def ssd_chunked_scan(x, dt, a_coef, bm, cm):
    bsz, seq, n_heads, hp = x.shape
    n_groups, n_state = bm.shape[2], bm.shape[3]
    r = n_heads // n_groups
    lc = SSM_CHUNK
    nc = seq // lc
    xc = (x.astype(jnp.float32) * dt[..., None]).reshape(bsz, nc, lc, n_groups, r, hp)
    ac = (dt * a_coef).reshape(bsz, nc, lc, n_groups, r)
    bc = bm.astype(jnp.float32).reshape(bsz, nc, lc, n_groups, n_state)
    cc = cm.astype(jnp.float32).reshape(bsz, nc, lc, n_groups, n_state)
    a_cum = jnp.cumsum(ac, axis=2)
    seg = a_cum[:, :, :, None] - a_cum[:, :, None, :]
    tril = jnp.tril(jnp.ones((lc, lc), dtype=bool))[None, None, :, :, None, None]
    decay = jnp.exp(jnp.where(tril, seg, -jnp.inf))
    cb = jnp.einsum('bclgn,bcsgn->bclsg', cc, bc)
    y_diag = jnp.einsum('bclsgr,bcsgrp->bclgrp', cb[..., None] * decay, xc)
    decay_to_end = jnp.exp(a_cum[:, :, -1:] - a_cum)
    states = jnp.einsum('bclgn,bclgrp->bcgrpn', bc, decay_to_end[..., None] * xc)
    chunk_decay = jnp.exp(a_cum[:, :, -1])

    def step(h, inp):
        st, dec = inp
        return h * dec[..., None, None] + st, h

    h0 = jnp.zeros((bsz, n_groups, r, hp, n_state), jnp.float32)
    _, h_in = lax.scan(step, h0, (jnp.swapaxes(states, 0, 1), jnp.swapaxes(chunk_decay, 0, 1)))
    h_in = jnp.swapaxes(h_in, 0, 1)
    y_off = jnp.einsum('bclgn,bcgrpn->bclgrp', cc, h_in) * jnp.exp(a_cum)[..., None]
    return (y_diag + y_off).reshape(bsz, seq, n_heads, hp)

def mamba2_heads(z, xbc, dt, conv_w, conv_b, dt_bias, a_log, d_skip, out_norm_g):
    bsz, seq, _ = z.shape
    xbc = jax.nn.silu(causal_depthwise_conv(xbc, conv_w, conv_b))
    xs, bm, cm = jnp.split(xbc, [SSM_D_INNER, SSM_D_INNER + SSM_GROUPS * SSM_D_STATE], axis=-1)
    dt = jax.nn.softplus(dt.astype(jnp.float32) + dt_bias.astype(jnp.float32))
    a_coef = -jnp.exp(a_log.astype(jnp.float32))
    xh = xs.reshape(bsz, seq, SSM_HEADS, SSM_HEAD_DIM)
    y = ssd_chunked_scan(xh, dt, a_coef,
                         bm.reshape(bsz, seq, SSM_GROUPS, SSM_D_STATE),
                         cm.reshape(bsz, seq, SSM_GROUPS, SSM_D_STATE))
    y = y + d_skip.astype(jnp.float32)[:, None] * xh.astype(jnp.float32)
    y = y.reshape(bsz, seq, SSM_D_INNER) * jax.nn.silu(z.astype(jnp.float32))
    return rms_norm(y, out_norm_g).astype(z.dtype)

def attn_ssd_mixer(h, w_in, q_norm_g, k_norm_g, sinks, conv_w, conv_b, dt_bias, a_log, d_skip,
                   out_norm_g, w_out):
    bsz, seq, _ = h.shape
    proj = h @ w_in
    cuts = np.cumsum([Q_COLS, KV_COLS, KV_COLS, SSM_D_INNER, SSM_CONV_CH]).tolist()
    q, k, v, z, xbc, dt = jnp.split(proj, cuts, axis=-1)
    q = rms_norm(q.reshape(bsz, seq, ATTN_HEADS, HEAD_DIM), q_norm_g)
    k = rms_norm(k.reshape(bsz, seq, ATTN_KV_HEADS, HEAD_DIM), k_norm_g)
    v = v.reshape(bsz, seq, ATTN_KV_HEADS, HEAD_DIM)
    y_attn = sliding_window_sink_attention(q, k, v, sinks)
    y_ssm = mamba2_heads(z, xbc, dt, conv_w, conv_b, dt_bias, a_log, d_skip, out_norm_g)
    return jnp.concatenate([y_attn, y_ssm], axis=-1) @ w_out

def conformer_conv_module(h, w_pw1, b_pw1, w_dw, b_dw, ln_g, ln_b, w_pw2, b_pw2):
    u = h @ w_pw1 + b_pw1
    u = u[..., :CONV_CH] * jax.nn.sigmoid(u[..., CONV_CH:])
    u = causal_depthwise_conv(u, w_dw, b_dw)
    u = jax.nn.silu(layer_norm(u, ln_g, ln_b))
    return u @ w_pw2 + b_pw2

def hierarchical_moe(h, w_group, b_group, w_expert, b_expert, w_gate_up, w_down):
    bsz, seq, dm = h.shape
    n_tok = bsz * seq
    xt = h.reshape(n_tok, dm)
    g_logits = (xt @ w_group).astype(jnp.float32) + b_group.astype(jnp.float32)
    g_sel = jnp.argmax(g_logits, axis=-1)
    g_w = jnp.take_along_axis(jax.nn.softmax(g_logits, axis=-1), g_sel[:, None], axis=-1)[:, 0]
    e_all = (xt @ w_expert).astype(jnp.float32).reshape(n_tok, MOE_GROUPS, MOE_EXPERTS_PER_GROUP)
    e_all = e_all + b_expert.astype(jnp.float32)[None]
    e_logits = jnp.take_along_axis(e_all, g_sel[:, None, None], axis=1)[:, 0]
    top_v, top_i = lax.top_k(e_logits, MOE_TOP_K)
    gate = (g_w[:, None] * jax.nn.softmax(top_v, axis=-1)).reshape(-1)
    eid = (g_sel[:, None] * MOE_EXPERTS_PER_GROUP + top_i).reshape(-1)
    n_slots = n_tok * MOE_TOP_K
    tok = jnp.arange(n_slots) // MOE_TOP_K
    order = jnp.argsort(eid)
    eid_s, tok_s, gate_s = eid[order], tok[order], gate[order]
    counts = jnp.bincount(eid, length=MOE_EXPERTS)
    starts = jnp.cumsum(counts) - counts
    padded = (counts + MOE_BLOCK - 1) // MOE_BLOCK * MOE_BLOCK
    pends = jnp.cumsum(padded)
    pstarts = pends - padded
    row = pstarts[eid_s] + (jnp.arange(n_slots) - starts[eid_s])
    n_rows = n_slots + MOE_EXPERTS * MOE_BLOCK
    n_blocks = n_rows // MOE_BLOCK
    buf = jnp.zeros((n_rows, dm), h.dtype).at[row].set(xt[tok_s])
    block_expert = jnp.minimum(
        jnp.searchsorted(pends, jnp.arange(n_blocks) * MOE_BLOCK, side='right'), MOE_EXPERTS - 1)

    def expert_block(args):
        xb, e = args
        gu = xb @ w_gate_up[e]
        return (jax.nn.silu(gu[:, :EXPERT_FF]) * gu[:, EXPERT_FF:]) @ w_down[e]

    out = lax.map(expert_block, (buf.reshape(n_blocks, MOE_BLOCK, dm), block_expert))
    y_s = out.reshape(n_rows, dm)[row] * gate_s[:, None].astype(h.dtype)
    y = jnp.zeros((n_tok, dm), h.dtype).at[tok_s].add(y_s)
    return y.reshape(bsz, seq, dm)

def setup_inputs(seed: int = 0) -> dict:
    key = jax.random.key(seed)
    ks = iter(jax.random.split(key, 48))

    def nrm(shape, scale):
        return jax.random.normal(next(ks), shape, jnp.float32) * scale

    def gain(shape):
        return 1.0 + nrm(shape, 0.05)

    ne, no = N_EVEN, N_ODD
    u = jax.random.uniform(next(ks), (ne, SSM_HEADS), jnp.float32)
    dt0 = jnp.exp(u * (np.log(0.1) - np.log(0.001)) + np.log(0.001)).astype(jnp.float32)
    dt_bias = dt0 + jnp.log(-jnp.expm1(-dt0))
    a_log = jnp.log(jax.random.uniform(next(ks), (ne, SSM_HEADS), jnp.float32, 1.0, 16.0))
    return {
        'x': nrm((BATCH, SEQ, D_MODEL), 1.0),
        'mix_norm_g': gain((ne, D_MODEL)),
        'w_in': nrm((ne, D_MODEL, IN_COLS), D_MODEL ** -0.5),
        'q_norm_g': gain((ne, HEAD_DIM)),
        'k_norm_g': gain((ne, HEAD_DIM)),
        'attn_sinks': nrm((ne, ATTN_HEADS), 1.0),
        'ssm_conv_w': nrm((ne, SSM_CONV, SSM_CONV_CH), SSM_CONV ** -0.5),
        'ssm_conv_b': nrm((ne, SSM_CONV_CH), 0.02),
        'ssm_dt_bias': dt_bias,
        'ssm_a_log': a_log,
        'ssm_d': gain((ne, SSM_HEADS)),
        'ssm_out_norm_g': gain((ne, SSM_D_INNER)),
        'w_out': nrm((ne, MIX_WIDTH, D_MODEL), MIX_WIDTH ** -0.5),
        'conv_norm_g': gain((no, D_MODEL)),
        'conv_w_pw1': nrm((no, D_MODEL, 2 * CONV_CH), D_MODEL ** -0.5),
        'conv_b_pw1': nrm((no, 2 * CONV_CH), 0.02),
        'conv_w_dw': nrm((no, CONV_KERNEL, CONV_CH), CONV_KERNEL ** -0.5),
        'conv_b_dw': nrm((no, CONV_CH), 0.02),
        'conv_ln_g': gain((no, CONV_CH)),
        'conv_ln_b': nrm((no, CONV_CH), 0.02),
        'conv_w_pw2': nrm((no, CONV_CH, D_MODEL), CONV_CH ** -0.5),
        'conv_b_pw2': nrm((no, D_MODEL), 0.02),
        'moe_norm_g': gain((DEPTH, D_MODEL)),
        'moe_w_group': nrm((DEPTH, D_MODEL, MOE_GROUPS), D_MODEL ** -0.5),
        'moe_b_group': nrm((DEPTH, MOE_GROUPS), 0.01),
        'moe_w_expert': nrm((DEPTH, D_MODEL, MOE_EXPERTS), D_MODEL ** -0.5),
        'moe_b_expert': nrm((DEPTH, MOE_GROUPS, MOE_EXPERTS_PER_GROUP), 0.01),
        'moe_w_gate_up': nrm((DEPTH, MOE_EXPERTS, D_MODEL, 2 * EXPERT_FF), D_MODEL ** -0.5),
        'moe_w_down': nrm((DEPTH, MOE_EXPERTS, EXPERT_FF, D_MODEL), EXPERT_FF ** -0.5),
    }

def reference(x, mix_norm_g, w_in, q_norm_g, k_norm_g, attn_sinks, ssm_conv_w, ssm_conv_b,
              ssm_dt_bias, ssm_a_log, ssm_d, ssm_out_norm_g, w_out,
              conv_norm_g, conv_w_pw1, conv_b_pw1, conv_w_dw, conv_b_dw, conv_ln_g, conv_ln_b,
              conv_w_pw2, conv_b_pw2,
              moe_norm_g, moe_w_group, moe_b_group, moe_w_expert, moe_b_expert,
              moe_w_gate_up, moe_w_down):
    for layer in range(DEPTH):
        i = layer // 2
        if layer % 2 == 0:
            x = x + attn_ssd_mixer(rms_norm(x, mix_norm_g[i]), w_in[i], q_norm_g[i], k_norm_g[i],
                                   attn_sinks[i], ssm_conv_w[i], ssm_conv_b[i], ssm_dt_bias[i],
                                   ssm_a_log[i], ssm_d[i], ssm_out_norm_g[i], w_out[i])
        else:
            x = x + conformer_conv_module(rms_norm(x, conv_norm_g[i]), conv_w_pw1[i], conv_b_pw1[i],
                                          conv_w_dw[i], conv_b_dw[i], conv_ln_g[i], conv_ln_b[i],
                                          conv_w_pw2[i], conv_b_pw2[i])
        x = x + hierarchical_moe(rms_norm(x, moe_norm_g[layer]), moe_w_group[layer],
                                 moe_b_group[layer], moe_w_expert[layer], moe_b_expert[layer],
                                 moe_w_gate_up[layer], moe_w_down[layer])
    return x


_drawn_inputs = setup_inputs


def setup_inputs(seed=0):
    import zlib

    import numpy as np

    out = dict(_drawn_inputs(seed))
    spreads = {}
    factors = {'q_norm_g': 3.902,
     'k_norm_g': 2.784,
     'attn_sinks': 28.789,
     'conv_b_pw1': 2.983,
     'conv_ln_b': 4.027,
     'moe_b_group': 4.512,
     'moe_b_expert': 2.991,
     'conv_b_pw2': 2.735}
    for name, (base, spread) in spreads.items():
        noise = np.random.default_rng([zlib.crc32(name.encode()), seed]).standard_normal(out[name].shape)
        drawn = base * np.exp(spread * noise) if base else spread * noise
        out[name] = jnp.asarray(drawn.astype(out[name].dtype))
    for name, factor in factors.items():
        out[name] = (out[name] * factor).astype(out[name].dtype)
    return out
```

```python
from contextlib import ExitStack

import numpy as np

import concourse.bass as bass
import concourse.mybir as mybir
from concourse.alu_op_type import AluOpType as ALU

F32 = mybir.dt.float32
I32 = mybir.dt.int32
BF16 = mybir.dt.bfloat16
ACT = mybir.ActivationFunctionType
AX = mybir.AxisListType

P = 128
D = 1024
T = 1024
NT = T // P
KD = D // P
DH = 64
NH = 8
NKV = 2
NS = 8
DI = 512
CONV_CH = 1024
SCONV = 4
KC = CONV_CH // P
Q0, K0, Z0, X0, DT0 = 0, 512, 768, 1280, 2304
IN_COLS = 2312
TAPS = 31
HALO = TAPS - 1
NG, EG = 4, 8
NE = NG * EG
FF = 512
KF = FF // P
NR = NG + NE
NEG = -1.0e30
RMS_EPS = 1e-6
LN_EPS = 1e-5
MAX_OVER = 2 * T // P


class Link:

    def __init__(self, eng, sem, per=None):
        self.eng, self.sem, self.per, self.base, self.n = eng, sem, per, 0, 0

    def begin(self, turn):
        if self.per is not None and self.n:
            assert self.n == self.per, (self.n, self.per)
        self.base, self.n = turn * self.per, 0

    def __call__(self, ins):
        self.n += 1
        ins.then_inc(self.sem, 1)
        self.eng.wait_ge(self.sem, self.base + self.n)


def at(i, n=1):
    return bass.ds(i, n)


def wait(eng, sem, value):
    if not (isinstance(value, int) and value <= 0):
        eng.wait_ge(sem, value)


def semaphores(nc, ctx, suffix=""):
    made = []

    def clear():
        numbers = sorted(s.num for s in made)
        with nc.Block() as block:
            @block.gpsimd
            def _(pool):
                first = 0
                for n in range(1, len(numbers) + 1):
                    if n == len(numbers) or numbers[n] != numbers[n - 1] + 1:
                        pool.sem_clear(range(numbers[first], numbers[n - 1] + 1))
                        first = n

    ctx.callback(clear)

    def make(name):
        made.append(ctx.enter_context(nc.semaphore(name + suffix)))
        return made[-1]
    return make


class Trunk:
    def __init__(self, nc, ins, out):
        self.nc, self.i, self.out = nc, ins, out

    def build(self):
        nc = self.nc
        with ExitStack() as ctx:
            self.ctx = ctx
            sb = lambda name, shape, dt=F32: ctx.enter_context(nc.sbuf_tensor(name, shape, dt))
            self.x = sb("x_res", [P, NT, D])
            self.ident = sb("ident", [P, P])
            self.upper = sb("upper", [P, P])
            self.ones = sb("ones", [P, P])
            self.mhalf = sb("mhalf", [P, 16])
            self.ps = ctx.enter_context(nc.psum_tensor("ps", [P, 8, 512], F32))
            self.token_slot = nc.dram_tensor("token_slot", (P * NE + MAX_OVER * P, 1), I32).ap()
            self.hbuf = nc.dram_tensor("h_rows", (T, D), F32).ap()
            self.ybuf = nc.dram_tensor("y_rows", (2 * T, D), F32).ap()
            self.dma_sems = [{n: ctx.enter_context(nc.semaphore(f"{n}_{layer}")) for n in (
                "table_made", "gathered0", "gathered1", "stored0", "stored1", "over_gathered", "over_stored")} for layer in range(2)]
            mixer(self)
            moe(self, 0)
            conformer(self)
            moe(self, 1)


def mixer(k):
    nc, x, ident, upper, ones, mhalf, ps = k.nc, k.x, k.ident, k.upper, k.ones, k.mhalf, k.ps
    I = k.i
    with ExitStack() as ctx:
        sb = lambda name, shape, dt=F32: ctx.enter_context(nc.sbuf_tensor(name, shape, dt))
        sem = semaphores(nc, ctx)
        w_in = sb("w_in_sb", [P, KD, IN_COLS])
        w_out = sb("w_out_sb", [P, KD, D])
        g_in = sb("g_in", [P, KD])
        g_cat = sb("g_cat", [P, KD])
        g_q = sb("g_q", [P, 1])
        g_k = sb("g_k", [P, 1])
        sinks = sb("sinks", [P, NH])
        conv_w = sb("conv_w", [P, KC, SCONV])
        conv_b = sb("conv_b", [P, KC])
        dt_bias = sb("dt_bias", [P, NS])
        a_coef = sb("a_coef", [P, NS])
        d_skip = sb("d_skip", [P, NS])
        mask = sb("mask", [P, 2, 2 * P])
        prev_mask = sb("prev_mask", [P, P])
        ss = sb("ss", [P, NT])
        rstd = sb("rstd", [P, NT])
        hn = sb("hn", [P, D])
        hT = hn[:, :].rearrange("p (k t) -> p k t", k=KD)
        q_raw = sb("q_raw", [P, NH * DH])
        kvd = sb("kvd", [P, 264])
        sq = sb("sq", [P, 640])
        qk_ss = sb("qk_ss", [P, 10])
        qk_r = sb("qk_r", [P, 10])
        qn = q_raw
        kd = sb("kd", [P, NKV, 2, DH])
        qT = sb("qT", [P, 4, P])
        kT = sb("kT", [P, NKV, 2, P])
        v = sb("v", [P, 2, P])
        z = sb("z", [P, DI])
        zs = sb("zs", [P, DI])
        cb = sb("cb", [P, KC, SCONV - 1 + P])
        cv = sb("cv", [P, KC, P])
        sx = sb("sx", [P, KC, P])
        s = sb("s", [P, 2, 4, 2 * P])
        m = sb("m", [P, 2, 4])
        nm = sb("nm", [P, 2, 4])
        sinkm = sb("sinkm", [P, 2, 4])
        esink = sb("esink", [P, 2, 4])
        den = sb("den", [P, 2, 4])
        rden = sb("rden", [P, 2, 4])
        pT = s[:, :, :, :].rearrange("p g j k -> p g (j k)").rearrange("p g (s j q) -> p g s j q", s=2, j=4)
        t_dt = sb("t_dt", [P, 4, NS])
        dt = sb("dt", [P, 2, NS])
        a = sb("a", [P, NS])
        ua = sb("ua", [P, NS, P])
        acum = sb("acum", [P, NS])
        sm = sb("sm", [P, 3, NS])
        se = sb("se", [P, 3, NS])
        seg = sb("seg", [P, NS, P])
        dec = mt = seg
        cbm = sb("cbm", [P, 2, P])
        xdt = sb("xdt", [P, NS, DH])
        xde = sb("xde", [P, NS, DH])
        xskip = sb("xskip", [P, DI])
        btm = sb("btm", [P, 2 * P])
        state = sb("state", [P, NS, DH])
        y = sb("y", [P, NS, DH])
        y2 = y[:, :, :].rearrange("p h d -> p (h d)")
        y_ss = sb("y_ss", [P, 1])
        y_r = sb("y_r", [P, 1])
        ycat = sb("ycat", [P, D])
        yT = ycat[:, :].rearrange("p (k t) -> p k t", k=KD)

        x_loaded, w_loaded, small_loaded = sem("x_loaded"), sem("w_loaded"), sem("small_loaded")
        wo_loaded = sem("wo_loaded")
        consts, act_consts = sem("consts"), sem("act_consts")
        x_squared, rstd_ready, hn_ready, hT_ready = sem("x_squared"), sem("rstd_ready"), sem("hn_ready"), sem("hT_ready")
        hn_turned, qk_turned, q_projected, kv_projected = sem("hn_turned"), sem("qk_turned"), sem("q_proj"), sem("kv_proj")
        z_projected, x0_projected, x1_projected = sem("z_proj"), sem("x0_proj"), sem("x1_proj")
        xb_turned, cb_done, scored, rows_done, probs_turned = sem("xb_turned"), sem("cb_done"), sem("scored"), sem("rows_done"), sem("probs_turned")
        pv_done, y_done, y_turned, o_done = sem("pv_done"), sem("y_done"), sem("y_turned"), sem("o_done")
        q_out, kv_out, z_out, x0_out, x1_out = sem("q_out"), sem("kv_out"), sem("z_out"), sem("x0_out"), sem("x1_out")
        qT_ready, xb_out, cb_out, s_out, rows_out, pT_ready = sem("qT_ready"), sem("xb_out"), sem("cb_out"), sem("s_out"), sem("rows_out"), sem("pT_ready")
        pv_out, y_out, yT_ready, x_added = sem("pv_out"), sem("y_out"), sem("yT_ready"), sem("x_added")
        qk_squared, qk_summed, qk_rstd, qk_normed = sem("qk_squared"), sem("qk_summed"), sem("qk_rstd"), sem("qk_normed")
        maxed, sinkm_ready, probs_ready, esink_ready = sem("maxed"), sem("sinkm_ready"), sem("probs_ready"), sem("esink_ready")
        t_dt_ready, soft_ready, dt_ready, ua_ready = sem("t_dt_ready"), sem("soft_ready"), sem("dt_ready"), sem("ua_ready")
        seg_ready, dec_ready, mt_ready, xde_ready = sem("seg_ready"), sem("dec_ready"), sem("mt_ready"), sem("xde_ready")
        conv_done, sx_ready, zs_ready = sem("conv_done"), sem("sx_ready"), sem("zs_ready")
        y2_ready, y_squared, y_rstd, ycat_ready = sem("y2_ready"), sem("y_squared"), sem("y_rstd"), sem("ycat_ready")
        halo_ready, s_masked = sem("halo_ready"), sem("s_masked")
        v_ready, mask_ready = sem("v_ready"), sem("mask_ready")
        dve_link, act_link, pool_link = sem("dve_link"), sem("act_link"), sem("pool_link")
        waited = sem("waited")

        PJ0, PJ1, TR, S4, S5, B6, B7 = 0, 1, 2, 4, 5, 6, 7

        def turns(eng, turn):
            with eng.Fori(0, NT // 2 - 1) as it:
                for p in range(2):
                    turn(it * 2 + p, p, True, True, it)
            turn(NT - 2, 0, True, False, NT // 2 - 1)
            turn(NT - 1, 1, False, False, NT // 2 - 1)

        block = ctx.enter_context(nc.Block())

        @block.sync
        def _(sp):
            sp.dma_start(x[:, :, :], I["x"].rearrange("b (c p) d -> p (b c) d", p=P)).then_inc(x_loaded, 16)
            w = I["w_in"].rearrange("a (k p) n -> p (a k) n", p=P)
            for kk in range(0, KD, 2):
                sp.dma_start(w_in[:, kk:kk + 2, :], w[:, kk:kk + 2, :]).then_inc(w_loaded, 16)
            sp.dma_start(w_out[:, :, :], I["w_out"].rearrange("a (k p) n -> p (a k) n", p=P)).then_inc(wo_loaded, 16)

        @block.gpsimd
        def _(pool):
            link = Link(pool, pool_link)
            pool.memset(ident[:], 0.0).then_inc(consts, 1)
            pool.memset(upper[:], 1.0).then_inc(consts, 1)
            pool.memset(ones[:], 1.0).then_inc(consts, 1)
            pool.memset(mhalf[:], -0.5).then_inc(consts, 1)
            pool.memset(mask[:], 0.0).then_inc(consts, 1)
            pool.memset(prev_mask[:], 0.0).then_inc(consts, 1)
            pool.memset(state[:], 0.0).then_inc(consts, 1)
            pool.memset(kT[:], 0.0).then_inc(consts, 1)
            pool.memset(v[:], 0.0).then_inc(consts, 1)
            pool.memset(cb[:], 0.0).then_inc(consts, 1)
            pool.memset(g_cat[:], 1.0).then_inc(consts, 1)
            pool.wait_ge(consts, 11)
            aff = dict(fill=NEG, base=0, pattern=[[-1, P]], channel_multiplier=1)
            pool.affine_select(out=ident[:], in_=ident[:], compare_op=ALU.not_equal, fill=1.0, base=0,
                               pattern=[[-1, P]], channel_multiplier=1).then_inc(consts, 1)
            pool.affine_select(out=upper[:], in_=upper[:], compare_op=ALU.is_ge, fill=0.0, base=0,
                               pattern=[[1, P]], channel_multiplier=-1).then_inc(consts, 1)
            pool.affine_select(out=mask[:, 0, 0:P], in_=mask[:, 0, 0:P], compare_op=ALU.is_ge, **aff).then_inc(consts, 1)
            pool.affine_select(out=mask[:, 1, P:2 * P], in_=mask[:, 1, P:2 * P], compare_op=ALU.is_ge, **aff).then_inc(consts, 1)
            pool.memset(mask[:, 0, P:2 * P], NEG).then_inc(consts, 1)
            seen = dict(fill=NEG, base=0, pattern=[[1, P]], channel_multiplier=-1)
            pool.affine_select(out=mask[:, 1, 0:P], in_=mask[:, 1, 0:P], compare_op=ALU.is_gt, **seen).then_inc(consts, 1)
            pool.affine_select(out=prev_mask[:], in_=prev_mask[:], compare_op=ALU.is_gt, **seen).then_inc(consts, 1)
            pool.wait_ge(consts, 18)
            pool.wait_ge(x_squared, NT)
            link(pool.tensor_scalar(ss[:], ss[:], 1.0 / D, RMS_EPS, ALU.mult, ALU.add))
            pool.tensor_tensor(rstd[:], ss[:], mhalf[:, 0:NT], ALU.pow).then_inc(rstd_ready, 1)
            pool.wait_ge(small_loaded, 16 * 15)
            pool.wait_ge(act_consts, 1)
            link(pool.tensor_scalar(a_coef[:], a_coef[:], -1.0, None, ALU.mult))
            pool.sem_inc(mask_ready, 1)

            def take_wait():
                pool.sem_inc(waited, 1)

            def qk_rstd_and_dt(c):
                pool.wait_ge(qk_summed, c + 1)
                take_wait()
                link(pool.tensor_scalar(qk_r[:], qk_ss[:], 1.0 / DH, RMS_EPS, ALU.mult, ALU.add))
                pool.tensor_tensor(qk_r[:], qk_r[:], mhalf[:, 0:10], ALU.pow).then_inc(qk_rstd, 1)
                pool.wait_ge(kv_out, c + 1)
                pool.tensor_tensor(t_dt[:, 0, :], kvd[:, 256:264], dt_bias[:], ALU.add).then_inc(t_dt_ready, 1)
                pool.wait_ge(t_dt_ready, c + 1)
                take_wait()
                link(pool.tensor_scalar(t_dt[:, 3, :], t_dt[:, 0, :], 0.0, None, ALU.max))
                pool.wait_ge(soft_ready, c + 1)

            def dt_and_rows(c, p):
                pool.tensor_tensor(dt[:, p, :], t_dt[:, 3, :], t_dt[:, 2, :], ALU.add).then_inc(dt_ready, 1)
                pool.wait_ge(dt_ready, c + 1)
                link(pool.tensor_tensor(a[:], dt[:, p, :], a_coef[:], ALU.mult))
                pool.tensor_tensor(ua[:], upper[:, :].unsqueeze(1).to_broadcast([P, NS, P]),
                                   a[:, :].unsqueeze(2).to_broadcast([P, NS, P]), ALU.mult).then_inc(ua_ready, 1)

            qk_rstd_and_dt(0)
            dt_and_rows(0, 0)
            pool.tensor_copy(v[:, 0, :], kvd[:, P:2 * P]).then_inc(v_ready, 1)
            first = link.n

            def turn(c, p, nxt, nxt2, it):
                link.base, link.n = c * TURN_LINKS_POOL + first, 0
                pool.wait_ge(dec_ready, c + 1)
                pool.wait_ge(cb_out, c + 1)
                pool.tensor_tensor(mt[:, 0:4, :], dec[:, 0:4, :], cbm[:, 0:1, :].to_broadcast([P, 4, P]), ALU.mult).then_inc(mt_ready, 1)
                pool.tensor_tensor(mt[:, 4:8, :], dec[:, 4:8, :], cbm[:, 1:2, :].to_broadcast([P, 4, P]), ALU.mult).then_inc(mt_ready, 1)
                pool.wait_ge(xb_out, 2 * c + 2)
                pool.tensor_tensor(xde[:], xdt[:], se[:, 1, :].unsqueeze(2).to_broadcast([P, NS, DH]), ALU.mult).then_inc(xde_ready, 1)
                if nxt:
                    qk_rstd_and_dt(c + 1)
                    pool.wait_ge(rows_done, c + 1)
                    dt_and_rows(c + 1, 1 - p)
                    pool.wait_ge(pv_done, c + 1)
                    take_wait()
                    pool.tensor_copy(v[:, 1 - p, :], kvd[:, P:2 * P]).then_inc(v_ready, 1)
                if p == 0:
                    pool.wait_ge(s_out, 2 * c + 2)
                    take_wait()
                    pool.tensor_copy(mask[:, 0, P:2 * P], prev_mask[:]).then_inc(mask_ready, 1)
                pool.wait_ge(y_squared, c + 1)
                take_wait()
                link(pool.tensor_scalar(y_r[:], y_ss[:], 1.0 / DI, RMS_EPS, ALU.mult, ALU.add))
                pool.tensor_tensor(y_r[:], y_r[:], mhalf[:, 0:1], ALU.pow).then_inc(y_rstd, 1)
                if nxt:
                    assert link.n == TURN_LINKS_POOL, link.n

            TURN_LINKS_POOL = 4
            turns(pool, turn)

        @block.scalar
        def _(act):
            act.wait_ge(consts, 18)
            col = lambda name, n: I[name].rearrange("a (k p) -> p (a k)", p=P)
            with nc.allow_non_contiguous_dma(reason="small per-channel vectors"):
                small = [(g_in[:], col("mix_norm_g", D)),
                         (g_cat[:, 4:8], col("ssm_out_norm_g", DI)),
                         (g_q[0:DH, :], I["q_norm_g"].rearrange("a d -> d a")),
                         (g_q[DH:P, :], I["q_norm_g"].rearrange("a d -> d a")),
                         (g_k[0:DH, :], I["k_norm_g"].rearrange("a d -> d a")),
                         (g_k[DH:P, :], I["k_norm_g"].rearrange("a d -> d a")),
                         (conv_b[:], col("ssm_conv_b", CONV_CH))]
                small += [(conv_w[:, :, j], I["ssm_conv_w"][0, j, :].rearrange("(k p) -> p k", p=P)) for j in range(SCONV)]
                for dst, name in ((sinks, "attn_sinks"), (dt_bias, "ssm_dt_bias"), (a_coef, "ssm_a_log"), (d_skip, "ssm_d")):
                    small.append((dst[:], I[name][0, :].partition_broadcast(P)))
                for dst, src in small:
                    act.dma_start(dst, src).then_inc(small_loaded, 16)
            act.wait_ge(x_loaded, 16)
            cb_flat = sx[:, :, :].rearrange("p k t -> p (k t)")
            for i in range(NT):
                if i:
                    act.wait_ge(x_squared, i)
                act.activation(cb_flat, x[:, i, :], ACT.Square,
                               accum_out=ss[:, i:i + 1]).then_inc(x_squared, 1)
            act.wait_ge(small_loaded, 16 * 15)
            act.activation(a_coef[:], a_coef[:], ACT.Exp).then_inc(act_consts, 1)

            def q_evacuate(c):
                act.wait_ge(q_projected, c + 1)
                if not (isinstance(c, int) and c == 0):
                    act.wait_ge(qk_turned, c)
                act.activation(q_raw[:], ps[:, PJ0, :], ACT.Copy).then_inc(q_out, 1)
                act.wait_ge(q_out, c + 1)
                act.activation(sq[:, 0:512], q_raw[:], ACT.Square).then_inc(qk_squared, 1)

            def kv_evacuate(c):
                act.wait_ge(kv_projected, c + 1)
                if not (isinstance(c, int) and c == 0):
                    act.wait_ge(v_ready, c)
                    act.wait_ge(dt_ready, c)
                act.activation(kvd[:], ps[:, PJ1, 0:264], ACT.Copy).then_inc(kv_out, 1)
                act.wait_ge(kv_out, c + 1)
                act.activation(sq[:, 512:640], kvd[:, 0:P], ACT.Square).then_inc(qk_squared, 1)

            def z_evacuate(c):
                act.wait_ge(z_projected, c + 1)
                act.activation(z[:], ps[:, PJ0, :], ACT.Copy).then_inc(z_out, 1)

            def x_evacuate(c, p, half):
                done, out = (x0_projected, x0_out) if half == 0 else (x1_projected, x1_out)
                bank = PJ1 if half == 0 else PJ0
                act.wait_ge(done, c + 1)
                if not (isinstance(c, int) and c == 0):
                    act.wait_ge(halo_ready, c)
                act.activation(cb[:, 4 * half:4 * half + 4, SCONV - 1:], ps[:, bank, :].rearrange("p (k t) -> p k t", k=4),
                               ACT.Copy).then_inc(out, 1)

            def softplus(c):
                act.wait_ge(t_dt_ready, c + 1)
                link(act.activation(t_dt[:, 1, :], t_dt[:, 0, :], ACT.Abs))
                link(act.activation(t_dt[:, 2, :], t_dt[:, 1, :], ACT.Exp, scale=-1.0))
                act.activation(t_dt[:, 2, :], t_dt[:, 2, :], ACT.Ln, bias=1.0).then_inc(soft_ready, 1)

            def silus(c, p):
                act.wait_ge(z_out, c + 1)
                if not (isinstance(c, int) and c == 0):
                    act.wait_ge(y2_ready, c)
                act.activation(zs[:], z[:], ACT.Silu).then_inc(zs_ready, 1)
                act.wait_ge(conv_done, 32 * (c + 1))
                if not (isinstance(c, int) and c == 0):
                    act.wait_ge(y_done, c)
                act.activation(sx[:, :, :], cv[:], ACT.Silu).then_inc(sx_ready, 1)

            link = Link(act, act_link, 2)
            link.begin(0)
            q_evacuate(0)
            kv_evacuate(0)
            softplus(0)
            z_evacuate(0)
            act.wait_ge(consts, 18)
            x_evacuate(0, 0, 0)
            x_evacuate(0, 0, 1)
            silus(0, 0)

            def probs(c, g):
                act.wait_ge(maxed, 2 * c + g + 1)
                for j in range(4):
                    act.activation(s[:, g, j, :], s[:, g, j, :], ACT.Exp, bias=nm[:, g, j:j + 1],
                                   accum_out=den[:, g, j:j + 1]).then_inc(probs_ready, 1)

            def probs_evacuate(c, g):
                act.wait_ge(probs_turned, 2 * c + g + 1)
                for slot in range(2):
                    act.activation(pT[:, g, slot, :, :].rearrange("p j q -> p (j q)"), ps[:, TR + slot, :],
                                   ACT.Copy).then_inc(pT_ready, 1)

            def turn(c, p, nxt, nxt2, it):
                link.base, link.n = 2 * c + 2, 0
                if nxt:
                    q_evacuate(c + 1)
                act.wait_ge(xb_turned, c + 1)
                act.activation(btm[:], ps[:, TR + 1, 0:256], ACT.Copy).then_inc(xb_out, 1)
                probs(c, 0)
                if nxt:
                    kv_evacuate(c + 1)
                act.wait_ge(seg_ready, c + 1)
                act.activation(se[:], sm[:], ACT.Exp).then_inc(esink_ready, 1)
                act.activation(dec[:], seg[:], ACT.Exp).then_inc(dec_ready, 1)
                probs(c, 1)
                act.activation(esink[:], sinkm[:], ACT.Exp).then_inc(esink_ready, 1)
                if nxt:
                    z_evacuate(c + 1)
                probs_evacuate(c, 0)
                if nxt:
                    softplus(c + 1)
                    x_evacuate(c + 1, 1 - p, 0)
                probs_evacuate(c, 1)
                act.wait_ge(y2_ready, c + 1)
                act.activation(xskip[:], y2[:], ACT.Square, accum_out=y_ss[:]).then_inc(y_squared, 1)
                if nxt:
                    x_evacuate(c + 1, 1 - p, 1)
                    silus(c + 1, 1 - p)

            turns(act, turn)

        @block.vector
        def _(dve):
            dve.wait_ge(rstd_ready, 1)

            def normalise(c, p):
                dve.tensor_scalar(hn[:, :].unsqueeze(1), x[:, at(c), :], rstd[:, at(c)], None, ALU.mult).then_inc(hn_ready, 1)

            def hT_evacuate(c, p):
                dve.wait_ge(hn_turned, c + 1)
                for half in range(2):
                    dve.tensor_tensor(hT[:, 4 * half:4 * half + 4, :], ps[:, TR + half, :].rearrange("p (k t) -> p k t", k=4),
                                      g_in[:, 4 * half:4 * half + 4].unsqueeze(2).to_broadcast([P, 4, P]), ALU.mult).then_inc(hT_ready, 1)

            def qk_norm(c):
                dve.wait_ge(qk_squared, 2 * c + 2)
                dve.tensor_reduce(qk_ss[:], sq[:].rearrange("p (h d) -> p h d", d=DH), AX.X, ALU.add).then_inc(qk_summed, 1)
                dve.wait_ge(qk_rstd, c + 1)
                dve.tensor_tensor(qn[:].rearrange("p (h d) -> p h d", d=DH), q_raw[:].rearrange("p (h d) -> p h d", d=DH),
                                  qk_r[:, 0:8].unsqueeze(2).to_broadcast([P, NH, DH]), ALU.mult).then_inc(qk_normed, 1)
                for g in range(NKV):
                    ins = dve.tensor_scalar(kd[:, g, :, :], kvd[:, g * DH:(g + 1) * DH].unsqueeze(1).to_broadcast([P, 2, DH]),
                                            qk_r[:, 8 + g:9 + g], None, ALU.mult)
                ins.then_inc(qk_normed, 1)

            def convolve(c, p, half):
                dve.wait_ge(x0_out if half == 0 else x1_out, c + 1)
                tiles = range(4 * half, 4 * half + 4)
                for j in range(SCONV):
                    for t in tiles:
                        src, w = cb[:, t, j:j + P], conv_w[:, t, j:j + 1]
                        if j == 0:
                            ins = dve.tensor_scalar(cv[:, t, :], src, w, conv_b[:, t:t + 1], ALU.mult, ALU.add)
                        else:
                            ins = dve.scalar_tensor_tensor(out=cv[:, t, :], in0=src, scalar=w, in1=cv[:, t, :], op0=ALU.mult, op1=ALU.add)
                        ins.then_inc(conv_done, 1)
                    if j < SCONV - 1:
                        dve.wait_ge(conv_done, 32 * c + 16 * half + 4 * (j + 1))

            def halo(c, p):
                dve.wait_ge(conv_done, 32 * (c + 1))
                dve.tensor_copy(cb[:, :, 0:SCONV - 1], cb[:, :, P:P + SCONV - 1]).then_inc(halo_ready, 1)

            link = Link(dve, dve_link)
            normalise(0, 0)
            dve.wait_ge(small_loaded, 16 * 15)
            hT_evacuate(0, 0)
            qk_norm(0)
            convolve(0, 0, 0)
            convolve(0, 0, 1)
            halo(0, 0)
            dve.wait_ge(x1_projected, 1)
            normalise(1, 1)
            BEFORE, TURN = 0, 13

            def scores(c, p, g):
                dve.wait_ge(scored, 2 * c + g + 1)
                for b in range(2):
                    dve.tensor_tensor(s[:, g, 2 * b:2 * b + 2, :], ps[:, S4 + b, :].rearrange("p (j q) -> p j q", j=2),
                                      mask[:, p:p + 1, :].to_broadcast([P, 2, 2 * P]), ALU.add).then_inc(s_masked, 1)
                dve.wait_ge(s_masked, 4 * c + 2 * g + 2)
                dve.tensor_reduce(m[:, g, :], s[:, g, :, :], AX.X, ALU.max).then_inc(s_out, 1)
                dve.wait_ge(s_out, 2 * c + g + 1)
                link(dve.tensor_tensor(m[:, g, :].rearrange("p (b j) -> p b j", b=2), m[:, g, :].rearrange("p (b j) -> p b j", b=2),
                                       sinks[:, 4 * g:4 * g + 4].rearrange("p (j b) -> p b j", b=2), ALU.max))
                dve.tensor_tensor(sinkm[:, g, :].rearrange("p (b j) -> p b j", b=2), sinks[:, 4 * g:4 * g + 4].rearrange("p (j b) -> p b j", b=2),
                                  m[:, g, :].rearrange("p (b j) -> p b j", b=2), ALU.subtract).then_inc(sinkm_ready, 1)
                dve.tensor_scalar(nm[:, g, :], m[:, g, :], -1.0, None, ALU.mult).then_inc(maxed, 1)

            def turn(c, p, nxt, nxt2, it):
                link.base, link.n = c * TURN + BEFORE, 0
                if nxt:
                    hT_evacuate(c + 1, 1 - p)
                dve.wait_ge(qk_turned, c + 1)
                dve.tensor_scalar(qT[:], ps[:, S4, :].rearrange("p (j q) -> p j q", j=4), g_q[:, 0:1], DH ** -0.5, ALU.mult, ALU.mult).then_inc(qT_ready, 1)
                dve.tensor_scalar(kT[:, :, p, :], ps[:, S5, 0:256].rearrange("p (j q) -> p j q", j=2), g_k[:, 0:1], None, ALU.mult).then_inc(qT_ready, 1)
                dve.wait_ge(xb_turned, c + 1)
                dve.wait_ge(dt_ready, c + 1)
                xs = ps[:, TR, :].rearrange("p (h d) -> p h d", d=DH)
                link(dve.tensor_tensor(xskip[:].rearrange("p (h d) -> p h d", d=DH), xs, d_skip[:].unsqueeze(2).to_broadcast([P, NS, DH]), ALU.mult))
                dve.tensor_tensor(xdt[:], xs, dt[:, p, :].unsqueeze(2).to_broadcast([P, NS, DH]), ALU.mult).then_inc(xb_out, 1)
                dve.wait_ge(cb_done, c + 1)
                link(dve.tensor_copy(acum[:], ps[:, B6, 256:264]))
                dve.tensor_tensor(cbm[:], ps[:, B6, 0:256].rearrange("p (g l) -> p g l", g=2),
                                  upper[:, :].unsqueeze(1).to_broadcast([P, 2, P]), ALU.mult).then_inc(cb_out, 1)
                if p == 0:
                    dve.wait_ge(mask_ready, it + 1)
                scores(c, p, 0)
                dve.wait_ge(rows_done, c + 1)
                for g, bank in ((0, B7), (1, B6)):
                    rows = ps[:, bank, :].rearrange("p (h l) -> p h l", h=4)
                    dve.tensor_copy(sm[:, 2, 4 * g:4 * g + 4].unsqueeze(2), rows[:, :, P - 1:P]).then_inc(dve_link, 1)
                    for h in range(4):
                        dve.tensor_scalar(seg[:, 4 * g + h, :], rows[:, h, :], acum[:, 4 * g + h:4 * g + h + 1], 0.0,
                                          ALU.subtract, ALU.min).then_inc(rows_out, 1)
                link.n += 2
                dve.wait_ge(dve_link, link.base + link.n)
                link(dve.tensor_copy(sm[:, 0, :], acum[:]))
                dve.tensor_tensor(sm[:, 1, :], sm[:, 2, :], acum[:], ALU.subtract).then_inc(seg_ready, 1)
                scores(c, p, 1)
                if nxt:
                    qk_norm(c + 1)
                    convolve(c + 1, 1 - p, 0)
                dve.wait_ge(pv_done, c + 1)
                dve.wait_ge(esink_ready, 2 * c + 2)
                dve.wait_ge(probs_ready, 8 * c + 8)
                link(dve.tensor_tensor(den[:], den[:], esink[:], ALU.add))
                link(dve.reciprocal(rden[:], den[:]))
                for g in range(2):
                    heads = lambda ap: ap.rearrange("p (j b d) -> p b j d", b=2, d=DH)
                    dve.tensor_tensor(heads(ycat[:, 256 * g:256 * g + 256]), heads(ps[:, S4, 256 * g:256 * g + 256]),
                                      rden[:, g, :].rearrange("p (b j) -> p b j", b=2).unsqueeze(3).to_broadcast([P, 2, 2, DH]),
                                      ALU.mult).then_inc(pv_out, 1)
                dve.wait_ge(y_done, c + 1)
                bc = lambda ap: ap.unsqueeze(2).to_broadcast([P, NS, DH])
                hd = lambda ap: ap.rearrange("p (h d) -> p h d", d=DH)
                link(dve.tensor_tensor(y[:], hd(ps[:, B6, :]), bc(se[:, 0, :]), ALU.mult))
                link(dve.tensor_tensor(state[:], state[:], bc(se[:, 2, :]), ALU.mult))
                link(dve.tensor_tensor(y[:], hd(ps[:, S5, :]), y[:], ALU.add))
                dve.tensor_tensor(state[:], hd(ps[:, B7, :]), state[:], ALU.add).then_inc(y_out, 1)
                link(dve.tensor_tensor(y[:], y[:], hd(xskip[:]), ALU.add))
                dve.wait_ge(zs_ready, c + 1)
                dve.tensor_tensor(y2[:], y[:].rearrange("p h d -> p (h d)"), zs[:], ALU.mult).then_inc(y2_ready, 1)
                dve.wait_ge(y_rstd, c + 1)
                dve.tensor_scalar(ycat[:, DI:D], y2[:], y_r[:], None, ALU.mult).then_inc(ycat_ready, 1)
                if nxt:
                    convolve(c + 1, 1 - p, 1)
                    halo(c + 1, 1 - p)
                dve.wait_ge(y_turned, c + 1)
                for half in range(2):
                    dve.tensor_tensor(yT[:, 4 * half:4 * half + 4, :], ps[:, TR + half, :].rearrange("p (k t) -> p k t", k=4),
                                      g_cat[:, 4 * half:4 * half + 4].unsqueeze(2).to_broadcast([P, 4, P]), ALU.mult).then_inc(yT_ready, 1)
                if nxt2:
                    dve.wait_ge(x1_projected, c + 2)
                    normalise(c + 2, p)
                dve.wait_ge(o_done, c + 1)
                for half in range(2):
                    dve.tensor_tensor(x[:, at(c), 512 * half:512 * half + 512], ps[:, S4 + half:S4 + half + 1, :],
                                      x[:, at(c), 512 * half:512 * half + 512], ALU.add).then_inc(x_added, 1)
                if nxt:
                    assert link.n == TURN, link.n

            turns(dve, turn)

        @block.tensor
        def _(pe):
            def turn_hn(c, p):
                pe.wait_ge(hn_ready, c + 1)
                for j in range(KD):
                    mm = pe.transpose(ps[:, TR + j // 4, (j % 4) * P:(j % 4 + 1) * P], hn[:, j * P:(j + 1) * P], ident[:])
                mm.then_inc(hn_turned, 1)

            def project(c, p, bank, n0, n1, done, at0=0, last=True):
                for j in range(KD):
                    mm = pe.matmul(ps[:, bank, at0:at0 + n1 - n0], hT[:, j, :], w_in[:, j, n0:n1], start=(j == 0), stop=(j == KD - 1))
                if last:
                    mm.then_inc(done, 1)

            def project_x(c, p, half, bank, done):
                for t in range(4 * half, 4 * half + 4):
                    for j in range(KD):
                        mm = pe.matmul(ps[:, bank, (t % 4) * P:(t % 4 + 1) * P], w_in[:, j, X0 + t * P:X0 + (t + 1) * P], hT[:, j, :],
                                       start=(j == 0), stop=(j == KD - 1))
                mm.then_inc(done, 1)

            pe.wait_ge(consts, 18)
            turn_hn(0, 0)
            pe.wait_ge(hT_ready, 2)
            pe.wait_ge(w_loaded, 64)
            project(0, 0, PJ0, Q0, K0, q_projected)
            project(0, 0, PJ1, K0, Z0, kv_projected, last=False)
            project(0, 0, PJ1, DT0, IN_COLS, kv_projected, at0=256)
            pe.wait_ge(q_out, 1)
            project(0, 0, PJ0, Z0, X0, z_projected)
            pe.wait_ge(kv_out, 1)
            project_x(0, 0, 0, PJ1, x0_projected)
            pe.wait_ge(z_out, 1)
            project_x(0, 0, 1, PJ0, x1_projected)
            pe.wait_ge(wo_loaded, 16)

            def scores(c, g):
                for h in range(4 * g, 4 * g + 4):
                    r = slice(DH * (h % 2), DH * (h % 2) + DH)
                    mm = pe.matmul(ps[:, S4 + h % 2, (h % 4 // 2) * 256:(h % 4 // 2) * 256 + 256], qT[r, h // 2, :],
                                   kT[r, g, :, :].rearrange("p s t -> p (s t)"), start=True, stop=True)
                mm.then_inc(scored, 1)

            def turn_probs(c, g):
                pe.wait_ge(probs_ready, 8 * c + 4 * g + 4)
                for slot in range(2):
                    for j in range(4):
                        mm = pe.transpose(ps[:, TR + slot, j * P:(j + 1) * P], s[:, g, j, slot * P:(slot + 1) * P], ident[:])
                mm.then_inc(probs_turned, 1)

            def turn(c, p, nxt, nxt2, it):
                if nxt:
                    turn_hn(c + 1, 1 - p)
                pe.wait_ge(qk_normed, 2 * c + 2)
                for j in range(4):
                    pe.transpose(ps[:, S4, j * P:(j + 1) * P], qn[:, j * P:(j + 1) * P], ident[:])
                for g in range(NKV):
                    mm = pe.transpose(ps[:, S5, g * P:(g + 1) * P], kd[:, g, :, :].rearrange("p a d -> p (a d)"), ident[:])
                mm.then_inc(qk_turned, 1)
                if nxt:
                    pe.wait_ge(x1_out, c + 1)
                    pe.wait_ge(hT_ready, 2 * c + 4)
                    project(c + 1, 1 - p, PJ0, Q0, K0, q_projected)
                pe.wait_ge(sx_ready, c + 1)
                for t in range(6):
                    mm = pe.transpose(ps[:, TR + t // 4, (t % 4) * P:(t % 4 + 1) * P], sx[:, t, :], ident[:])
                mm.then_inc(xb_turned, 1)
                pe.wait_ge(ua_ready, c + 1)
                for g in range(2):
                    pe.matmul(ps[:, B6, g * P:(g + 1) * P], sx[:, 4 + g, :], sx[:, 6 + g, :], start=True, stop=True)
                pe.matmul(ps[:, B6, 256:264], upper[:], a[:], start=True, stop=True).then_inc(cb_done, 1)
                pe.wait_ge(qT_ready, 2 * c + 2)
                scores(c, 0)
                if nxt:
                    pe.wait_ge(x0_out, c + 1)
                    project(c + 1, 1 - p, PJ1, K0, Z0, kv_projected, last=False)
                    project(c + 1, 1 - p, PJ1, DT0, IN_COLS, kv_projected, at0=256)
                pe.wait_ge(cb_out, c + 1)
                pe.matmul(ps[:, B7, :], ones[:], ua[:, 0:4, :].rearrange("p h l -> p (h l)"), start=True, stop=True)
                pe.matmul(ps[:, B6, :], ones[:], ua[:, 4:8, :].rearrange("p h l -> p (h l)"), start=True, stop=True).then_inc(rows_done, 1)
                pe.wait_ge(s_out, 2 * c + 1)
                scores(c, 1)
                if nxt:
                    pe.wait_ge(q_out, c + 2)
                    project(c + 1, 1 - p, PJ0, Z0, X0, z_projected)
                pe.wait_ge(xb_out, 2 * c + 2)
                turn_probs(c, 0)
                if nxt:
                    pe.wait_ge(kv_out, c + 2)
                    project_x(c + 1, 1 - p, 0, PJ1, x0_projected)
                pe.wait_ge(pT_ready, 4 * c + 2)
                turn_probs(c, 1)
                pe.wait_ge(s_out, 2 * c + 2)
                pe.wait_ge(v_ready, c + 1)
                pe.wait_ge(pT_ready, 4 * c + 4)
                for h in range(NH):
                    g, j = h // 4, (h % 2) * 2 + h % 4 // 2
                    for slot in range(2):
                        mm = pe.matmul(ps[:, S4, h * DH:(h + 1) * DH], pT[:, g, slot, j, :], v[:, slot, g * DH:(g + 1) * DH],
                                       start=(slot == 0), stop=(slot == 1))
                mm.then_inc(pv_done, 1)
                pe.wait_ge(mt_ready, 2 * c + 2)
                for h in range(NS):
                    pe.matmul(ps[:, S5, h * DH:(h + 1) * DH], mt[:, h, :], xdt[:, h, :], start=True, stop=True)
                pe.wait_ge(rows_out, 8 * c + 8)
                for g in range(2):
                    pe.matmul(ps[:, B6, g * 256:(g + 1) * 256], sx[:, 6 + g, :], state[:, 4 * g:4 * g + 4, :].rearrange("p h d -> p (h d)"), start=True, stop=True)
                pe.wait_ge(xde_ready, c + 1)
                for g in range(2):
                    mm = pe.matmul(ps[:, B7, g * 256:(g + 1) * 256], btm[:, g * P:(g + 1) * P], xde[:, 4 * g:4 * g + 4, :].rearrange("p h d -> p (h d)"), start=True, stop=True)
                mm.then_inc(y_done, 1)
                if nxt:
                    pe.wait_ge(z_out, c + 2)
                    project_x(c + 1, 1 - p, 1, PJ0, x1_projected)
                pe.wait_ge(ycat_ready, c + 1)
                pe.wait_ge(pv_out, 2 * c + 2)
                for j in range(KD):
                    mm = pe.transpose(ps[:, TR + j // 4, (j % 4) * P:(j % 4 + 1) * P], ycat[:, j * P:(j + 1) * P], ident[:])
                mm.then_inc(y_turned, 1)
                pe.wait_ge(yT_ready, 2 * c + 2)
                pe.wait_ge(y_out, c + 1)
                for half in range(2):
                    for j in range(KD):
                        mm = pe.matmul(ps[:, S4 + half, :], yT[:, j, :], w_out[:, j, 512 * half:512 * half + 512], start=(j == 0), stop=(j == KD - 1))
                mm.then_inc(o_done, 1)
                if nxt:
                    pe.wait_ge(x_added, 2 * c + 2)

            turns(pe, turn)


def moe(k, layer):
    nc, x, ident, upper, ones, mhalf, ps, I = k.nc, k.x, k.ident, k.upper, k.ones, k.mhalf, k.ps, k.i
    PAD = 1 << 16
    with ExitStack() as outer:
        osb = lambda name, shape, dt=F32: outer.enter_context(nc.sbuf_tensor(f"{name}{layer}", shape, dt))
        osem = semaphores(nc, outer, str(layer))
        wgu = osb("wgu", [P, 2, KD, 2 * FF])
        wd = osb("wd", [P, 2, KF, D])
        g_moe = osb("g_moe", [P, KD])
        gates = osb("gates", [P, 2, NT])
        n_over = osb("n_over", [P, 1], I32)
        over_expert = osb("over_expert", [P, MAX_OVER], I32)
        hidx = osb("hidx", [P, NE], I32)
        yidx = osb("yidx", [P, NE], I32)
        gu_loaded = [osem(f"gu_loaded{p}_") for p in range(2)]
        wd_loaded = [osem(f"wd_loaded{p}_") for p in range(2)]
        w_gu = I["moe_w_gate_up"][layer].rearrange("e (k p) n -> e p k n", p=P)
        w_down = I["moe_w_down"][layer].rearrange("e (k p) n -> e p k n", p=P)

        def load_gate_up(sp, e, p):
            for half in range(2):
                sp.dma_start(wgu[:, p, 4 * half:4 * half + 4, :],
                             w_gu[at(e), :, 4 * half:4 * half + 4, :].rearrange("a p k n -> p (a k) n")).then_inc(gu_loaded[p], 16)

        def load_down(sp, e, p):
            sp.dma_start(wd[:, p, :, :], w_down[at(e)].rearrange("a p k n -> p (a k) n")).then_inc(wd_loaded[p], 16)

        with ExitStack() as ctx:
            sb = lambda name, shape, dt=F32: ctx.enter_context(nc.sbuf_tensor(f"{name}{layer}", shape, dt))
            sem = semaphores(nc, ctx, str(layer))
            w_router = sb("w_router", [P, KD, NR])
            b_router = sb("b_router", [P, NR])
            ss, rstd = sb("m_ss", [P, NT]), sb("m_rstd", [P, NT])
            sq = sb("m_sq", [P, D])
            h = sb("m_h", [P, 2, D])
            hT = sb("m_hT", [P, 2, KD, P])
            L = sb("logits", [P, NT, NR])
            strict = sb("strict", [P, P])
            desc = sb("desc", [P, NE])
            eid = sb("eid", [P, NE])
            blocks = sb("blocks", [P, MAX_OVER])
            iota_i = sb("iota_i", [P, NE], I32)
            slot_ids = sb("slot_ids", [P, 2, NT], I32)
            pad = sb("pad", [P, (P * NE + MAX_OVER * P) // P], I32)
            gm, gw, wm = sb("gm", [P, NT]), sb("gw", [P, NT]), sb("wm", [P, NT])
            ge, go = sb("ge", [P, NT, NG]), sb("go", [P, NT, NG])
            E, W = sb("E", [P, NT, NE]), sb("W", [P, NT, NE])
            M = [sb("M1_", [P, NT, NE]), sb("M2_", [P, NT, NE])]
            both = sb("both", [P, NT, NE])
            top = [sb("top1_", [P, NT]), sb("top2_", [P, NT])]
            ex, den = sb("ex", [P, NT]), sb("m_den", [P, NT])
            total = sb("total", [P, NT, NE])
            rank = sb("rank", [P, NT, NE])
            pre = sb("pre", [P, NT + 1, NE])
            extra, incl = sb("extra", [P, NE]), sb("incl", [P, NE])
            one_row = sb("one_row", [P, NE])
            shift = sb("shift", [P, NE])
            cmp = sb("cmp", [P, MAX_OVER, NE])
            oe = sb("oe", [P, MAX_OVER])
            pos, posf = sb("pos", [P, 2, NT], I32), sb("posf", [P, 2, NT])
            hi = sb("hi", [P, NE])

            small_loaded, squared, rstd_ready = sem("m_small"), sem("m_squared"), sem("m_rstd_ready")
            h_ready, h_turned, hT_ready, routed, logits_ready = sem("m_h_ready"), sem("m_turned"), sem("m_hT_ready"), sem("m_routed"), sem("m_logits")
            h_stored = [sem("h_stored0_"), sem("h_stored1_")]
            consts, ge_in, ge_out, ex_in, ex_out = sem("m_consts"), sem("ge_in"), sem("ge_out"), sem("ex_in"), sem("ex_out")
            both_ready, ranked, pos_ready, padded, table_read = sem("both_ready"), sem("ranked"), sem("pos_ready"), sem("padded"), sem("table_read")
            table_made = k.dma_sems[layer]["table_made"]
            dve_link, pool_link = sem("m_dve_link"), sem("m_pool_link")

            def turns(eng, turn):
                with eng.Fori(0, NT // 2 - 1) as it:
                    for p in range(2):
                        turn(it * 2 + p, p, True, it)
                for p in range(2):
                    turn(NT - 2 + p, p, False, NT // 2 - 1)

            block = ctx.enter_context(nc.Block())

            @block.sync
            def _(sp):
                with nc.allow_non_contiguous_dma(reason="router weights and a gain by channel"):
                    sp.dma_start(w_router[:, :, 0:NG], I["moe_w_group"][layer].rearrange("(k p) n -> p k n", p=P)).then_inc(small_loaded, 16)
                    sp.dma_start(w_router[:, :, NG:NR], I["moe_w_expert"][layer].rearrange("(k p) n -> p k n", p=P)).then_inc(small_loaded, 16)
                    sp.dma_start(g_moe[:], I["moe_norm_g"][layer].rearrange("(k p) -> p k", p=P)).then_inc(small_loaded, 16)
                sp.dma_start(b_router[:, 0:NG], I["moe_b_group"][layer].partition_broadcast(P)).then_inc(small_loaded, 16)
                sp.dma_start(b_router[:, NG:NR], I["moe_b_expert"][layer].rearrange("g e -> (g e)").partition_broadcast(P)).then_inc(small_loaded, 16)
                sp.wait_ge(consts, 1)
                sp.dma_start(k.token_slot.rearrange("(p n) a -> p (n a)", p=P), pad[:]).then_inc(padded, 16)
                def turn(i, p, more, it):
                    sp.wait_ge(h_ready, i + 1)
                    sp.dma_start(k.hbuf[bass.ds(i * P, P), :], h[:, p, :]).then_inc(h_stored[p], 16)
                turns(sp, turn)
                for p in range(2):
                    load_gate_up(sp, p, p)
                    load_down(sp, p, p)
                for p in range(2):
                    sp.wait_ge(h_stored[p], 16 * NT // 2)
                sp.wait_ge(table_made, 16 * 2 * NT)
                sp.dma_start(yidx[:], k.token_slot[0:P * NE, :].rearrange("(p e) a -> p (e a)", p=P)).then_inc(table_read, 16)

            @block.scalar
            def _(act):
                for i in range(NT):
                    if i:
                        act.wait_ge(squared, i)
                    act.activation(sq[:], x[:, i, :], ACT.Square, accum_out=ss[:, i:i + 1]).then_inc(squared, 1)

                act.sem_inc(logits_ready, 2)

                def turn(i, p, more, it):
                    act.wait_ge(routed, i + 1)
                    act.activation(L[:, at(i), :], ps[:, 4 + p:5 + p, 0:NR], ACT.Copy).then_inc(logits_ready, 1)
                turns(act, turn)
                act.wait_ge(ge_in, 1)
                act.activation(ge[:], ge[:], ACT.Exp).then_inc(ge_out, 1)
                act.wait_ge(ex_in, 1)
                act.activation(ex[:], ex[:], ACT.Exp).then_inc(ex_out, 1)

            @block.gpsimd
            def _(pool):
                link = Link(pool, pool_link)
                pool.memset(pad[:], PAD).then_inc(consts, 1)
                pool.wait_ge(squared, NT)
                link(pool.tensor_scalar(ss[:], ss[:], 1.0 / D, RMS_EPS, ALU.mult, ALU.add))
                pool.tensor_tensor(rstd[:], ss[:], mhalf[:, 0:NT], ALU.pow).then_inc(rstd_ready, 1)
                link(pool.memset(strict[:], 1.0))
                link(pool.memset(one_row[:], 1.0))
                link(pool.affine_select(out=strict[:], in_=strict[:], compare_op=ALU.is_gt, fill=0.0, base=0,
                                        pattern=[[1, P]], channel_multiplier=-1))
                link(pool.iota(iota_i[:], [[1, NE]], base=0, channel_multiplier=0))
                link(pool.iota(slot_ids[:], [[T, 2], [P, NT]], base=0, channel_multiplier=1))
                link(pool.tensor_copy(eid[:], iota_i[:]))
                link(pool.tensor_copy(blocks[:], iota_i[:, 0:MAX_OVER]))
                pool.tensor_scalar(desc[:], eid[:], -1.0, float(NE), ALU.mult, ALU.add).then_inc(consts, 1)
                pool.wait_ge(padded, 16)
                pool.wait_ge(pos_ready, 1)
                for j in range(2):
                    for i in range(NT):
                        pool.indirect_dma_start(out=k.token_slot, out_offset=bass.IndirectOffsetOnAxis(ap=pos[:, j, i:i + 1], axis=0),
                                                in_=slot_ids[:, j, i:i + 1], in_offset=None).then_inc(table_made, 16)

            @block.tensor
            def _(pe):
                pe.wait_ge(small_loaded, 16 * 5)

                def turn(i, p, more, it):
                    pe.wait_ge(h_ready, i + 1)
                    for j in range(KD):
                        mm = pe.transpose(ps[:, 2 * p + j // 4, (j % 4) * P:(j % 4 + 1) * P], h[:, p, j * P:(j + 1) * P], ident[:])
                    mm.then_inc(h_turned, 1)
                    pe.wait_ge(hT_ready, 2 * i + 2)
                    pe.wait_ge(logits_ready, i + 1)
                    for j in range(KD):
                        mm = pe.matmul(ps[:, 4 + p, 0:NR], hT[:, p, j, :], w_router[:, j, :], start=(j == 0), stop=(j == KD - 1))
                    mm.then_inc(routed, 1)
                turns(pe, turn)
                pe.wait_ge(both_ready, 1)
                pe.wait_ge(consts, 2)
                flat = both[:].rearrange("p i e -> p (i e)")
                pe.matmul(ps[:, 6, 0:NT * NE], strict[:], flat, start=True, stop=True)
                pe.matmul(ps[:, 7, 0:NT * NE], ones[:], flat, start=True, stop=True).then_inc(ranked, 1)

            @block.vector
            def _(dve):
                link = Link(dve, dve_link)

                def normalise(i, p):
                    dve.tensor_scalar(h[:, p:p + 1, :], x[:, at(i), :], rstd[:, at(i)], None, ALU.mult).then_inc(h_ready, 1)

                dve.wait_ge(rstd_ready, 1)
                normalise(0, 0)
                normalise(1, 1)
                dve.wait_ge(small_loaded, 16 * 5)

                def turn(i, p, more, it):
                    dve.wait_ge(h_turned, i + 1)
                    for half in range(2):
                        dve.tensor_tensor(hT[:, p, 4 * half:4 * half + 4, :], ps[:, 2 * p + half, :].rearrange("p (k t) -> p k t", k=4),
                                          g_moe[:, 4 * half:4 * half + 4].unsqueeze(2).to_broadcast([P, 4, P]), ALU.mult).then_inc(hT_ready, 1)
                    if more:
                        dve.wait_ge(h_stored[p], it * 16 + 16)
                        normalise(i + 2, p)
                turns(dve, turn)

                tt, ts = dve.tensor_tensor, dve.tensor_scalar
                by_group = lambda ap: ap.unsqueeze(2).to_broadcast([P, NT, NG])
                by_expert = lambda ap: ap.unsqueeze(2).to_broadcast([P, NT, NE])
                in_tiles = lambda ap, n: ap.unsqueeze(1).to_broadcast([P, NT, n])
                dve.wait_ge(consts, 2)
                dve.wait_ge(logits_ready, NT + 2)
                link(tt(L[:], L[:], in_tiles(b_router[:], NR), ALU.add))
                G = L[:, :, 0:NG]
                link(dve.tensor_reduce(gm[:], G, AX.X, ALU.max))
                tt(ge[:], G, by_group(gm[:]), ALU.subtract).then_inc(ge_in, 1)
                link(tt(go[:], G, by_group(gm[:]), ALU.is_equal))
                link(tt(go[:], go[:], in_tiles(desc[:, 0:NG], NG), ALU.mult))
                link(dve.tensor_reduce(wm[:], go[:], AX.X, ALU.max))
                link(tt(go[:], go[:], by_group(wm[:]), ALU.is_equal))
                dve.wait_ge(ge_out, 1)
                link(dve.tensor_reduce(gw[:], ge[:], AX.X, ALU.add))
                link(dve.reciprocal(gw[:], gw[:]))
                link(ts(go[:], go[:], 1.0, -NEG, ALU.subtract, ALU.mult))
                link(tt(E[:].rearrange("p i (g e) -> p i g e", g=NG), L[:, :, NG:NR].rearrange("p i (g e) -> p i g e", g=NG),
                        go[:].unsqueeze(3).to_broadcast([P, NT, NG, EG]), ALU.add))
                for j in range(2):
                    link(dve.tensor_reduce(top[j][:], E[:], AX.X, ALU.max))
                    link(tt(W[:], E[:], by_expert(top[j][:]), ALU.is_equal))
                    link(tt(W[:], W[:], in_tiles(desc[:], NE), ALU.mult))
                    link(dve.tensor_reduce(wm[:], W[:], AX.X, ALU.max))
                    link(tt(M[j][:], W[:], by_expert(wm[:]), ALU.is_equal))
                    if j == 0:
                        link(dve.scalar_tensor_tensor(out=E[:], in0=M[0][:], scalar=2 * NEG, in1=E[:], op0=ALU.mult, op1=ALU.add))
                tt(both[:], M[0][:], M[1][:], ALU.add).then_inc(both_ready, 1)
                tt(ex[:], top[1][:], top[0][:], ALU.subtract).then_inc(ex_in, 1)
                dve.wait_ge(ex_out, 1)
                link(ts(den[:], ex[:], 1.0, None, ALU.add))
                link(dve.reciprocal(den[:], den[:]))
                link(tt(gates[:, 0, :], gw[:], den[:], ALU.mult))
                link(tt(gates[:, 1, :], gates[:, 0, :], ex[:], ALU.mult))
                dve.wait_ge(ranked, 1)
                link(dve.tensor_copy(total[:].rearrange("p i e -> p (i e)"), ps[:, 7, 0:NT * NE]))
                link(dve.memset(pre[:, 0, :], 0.0))
                for i in range(NT):
                    link(tt(pre[:, i + 1, :], pre[:, i, :], total[:, i, :], ALU.add))
                link(tt(rank[:], ps[:, 6, 0:NT * NE].rearrange("p (i e) -> p i e", i=NT), pre[:, 0:NT, :], ALU.add))
                counts = pre[:, NT, :]
                link(ts(extra[:], counts, float(P), None, ALU.is_gt))
                for j in range(2, T // P):
                    link(dve.scalar_tensor_tensor(out=extra[:], in0=counts, scalar=float(j * P), in1=extra[:], op0=ALU.is_gt, op1=ALU.add))
                link(dve.tensor_tensor_scan(incl[:], one_row[:], extra[:], 0.0, ALU.mult, ALU.add))
                link(dve.tensor_copy(n_over[:], incl[:, NE - 1:NE]))
                link(tt(cmp[:], incl[:].unsqueeze(1).to_broadcast([P, MAX_OVER, NE]), blocks[:].unsqueeze(2).to_broadcast([P, MAX_OVER, NE]), ALU.is_le))
                link(dve.tensor_reduce(oe[:], cmp[:], AX.X, ALU.add))
                link(ts(oe[:], oe[:], float(NE - 1), None, ALU.min))
                link(dve.tensor_copy(over_expert[:], oe[:]))
                link(tt(shift[:], incl[:], extra[:], ALU.subtract))
                link(ts(shift[:], shift[:], float(P), float(NE * P - P), ALU.mult, ALU.add))
                link(ts(W[:], rank[:], float(NE), None, ALU.mult))
                link(tt(W[:], W[:], in_tiles(eid[:], NE), ALU.add))
                link(tt(E[:], rank[:], in_tiles(shift[:], NE), ALU.add))
                link(tt(E[:], E[:], W[:], ALU.subtract))
                link(ts(rank[:], rank[:], float(P), None, ALU.is_ge))
                link(tt(E[:], E[:], rank[:], ALU.mult))
                link(tt(E[:], E[:], W[:], ALU.add))
                for j in range(2):
                    link(tt(W[:], M[j][:], E[:], ALU.mult))
                    link(dve.tensor_reduce(posf[:, j, :], W[:], AX.X, ALU.add))
                dve.tensor_copy(pos[:], posf[:]).then_inc(pos_ready, 1)
                dve.wait_ge(table_read, 16)
                link(ts(hi[:], yidx[:], float(T), float(-T), ALU.is_ge, ALU.mult))
                link(tt(hidx[:], yidx[:], hi[:], ALU.add))

        with ExitStack() as ctx:
            sb = lambda name, shape, dt=F32: ctx.enter_context(nc.sbuf_tensor(f"{name}{layer}", shape, dt))
            sem = semaphores(nc, ctx, str(layer))
            xg = sb("xg", [P, 2, D])
            xT = sb("xT", [P, 2, KD, P])
            sg = sb("sg", [P, FF])
            hh = sb("hh", [P, 2, KF, P])
            y = sb("my", [P, 2, D])
            ih, iy = sb("ih", [P, 2], I32), sb("iy", [P, 2], I32)
            over_slot = sb("over_slot", [P, 1], I32)
            over_h = sb("over_h", [P, 1])
            gathered = [k.dma_sems[layer]["gathered0"], k.dma_sems[layer]["gathered1"]]
            stored = [k.dma_sems[layer]["stored0"], k.dma_sems[layer]["stored1"]]
            o_gathered, o_stored = k.dma_sems[layer]["over_gathered"], k.dma_sems[layer]["over_stored"]
            zeroed, idx_ready, waited, sp_waited = sem("zeroed"), sem("idx_ready"), sem("e_waited"), sem("sp_waited")
            turned, xT_ready, gu_done, silu_ready, hh_ready, d_done, y_ready = (sem(n) for n in (
                "e_turned", "xT_ready", "gu_done", "silu_ready", "hh_ready", "d_done", "e_y_ready"))
            o_idx, o_index, o_turned, o_xT, o_gu, o_silu, o_hh, o_d, o_y, o_w = (sem(n) for n in (
                "o_idx", "o_index", "o_turned", "o_xT", "o_gu", "o_silu", "o_hh", "o_d", "o_y", "o_w"))
            y_loaded = [sem(f"y_loaded{i}_") for i in range(NT)]
            x_sum = sem("x_sum")
            out_done = sem("out_done")

            def turns(eng, turn):
                for q in range(2):
                    turn(1 + q, 1 - q, 0)
                with eng.Fori(1, NE // 2 - 1) as it:
                    for q in range(2):
                        turn(it * 2 + 1 + q, 1 - q, it)

            def turns_over(eng, turn):
                n = eng.value_load(n_over[0:1, 0:1], min_val=0, max_val=MAX_OVER)
                with eng.If(n > 0):
                    with eng.Fori(0, n) as j:
                        turn(j)

            block = ctx.enter_context(nc.Block())

            @block.sync
            def _(sp):
                def refill(e, p):
                    sp.wait_ge(gu_done, e + 2)
                    load_gate_up(sp, e + 3, 1 - p)
                    sp.wait_ge(d_done, e + 1)
                    load_down(sp, e + 2, p)

                sp.wait_ge(gu_done, 1)
                load_gate_up(sp, 2, 0)
                with sp.Fori(0, NE // 2 - 2) as it:
                    for p in range(2):
                        refill(it * 2 + p, p)
                refill(NE - 4, 0)
                sp.wait_ge(d_done, NE - 2)
                load_down(sp, NE - 1, 1)
                sp.wait_ge(gu_done, NE)
                sp.wait_ge(d_done, NE)
                for p in range(2):
                    sp.wait_ge(stored[p], 16 * (NE // 2))

                def over(j):
                    sp.dma_start(over_slot[:], k.token_slot[bass.ds(j * P + P * NE, P), :]).then_inc(o_idx, 16)
                    e = sp.value_load(over_expert[0:1, at(j)], min_val=0, max_val=NE - 1)
                    sp.dma_start(wgu[:, 0, :, :], w_gu[at(e)].rearrange("a p k n -> p (a k) n")).then_inc(o_w, 16)
                    sp.dma_start(wd[:, 0, :, :], w_down[at(e)].rearrange("a p k n -> p (a k) n")).then_inc(o_w, 16)
                    sp.wait_ge(o_stored, j * 16 + 16)
                    sp.sem_inc(sp_waited, 1)
                turns_over(sp, over)
                for i in range(NT):
                    for j in range(2):
                        sp.dma_start(wgu[:, j, i, :], k.ybuf[j * T + i * P:j * T + (i + 1) * P, :]).then_inc(y_loaded[i], 16)
                if layer == 1:
                    for i in range(NT):
                        sp.wait_ge(x_sum, 2 * i + 2)
                        sp.dma_start(k.out[0, i * P:(i + 1) * P, :], x[:, i, :]).then_inc(out_done, 16)
                    sp.wait_ge(out_done, 16 * NT)

            @block.gpsimd
            def _(pool):
                pool.memset(xg[:], 0.0).then_inc(zeroed, 1)
                pool.wait_ge(zeroed, 1)

                last_h, last_y = pool.to_reg(T - 1), pool.to_reg(2 * T - 1)

                def take_wait():
                    pool.sem_inc(waited, 1)

                def gather(e, p, n):
                    pool.tensor_copy(ih[:, p:p + 1], hidx[:, at(e)]).then_inc(idx_ready, 1)
                    pool.wait_ge(idx_ready, n)
                    take_wait()
                    pool.indirect_dma_start(out=xg[:, p, :], out_offset=None, in_=k.hbuf,
                                            in_offset=bass.IndirectOffsetOnAxis(ap=ih[:, p:p + 1], axis=0),
                                            bounds_check=last_h, oob_is_err=False).then_inc(gathered[p], 16)

                def scatter(e, p, n):
                    pool.tensor_copy(iy[:, p:p + 1], yidx[:, at(e)]).then_inc(idx_ready, 1)
                    pool.wait_ge(idx_ready, n)
                    pool.wait_ge(y_ready, e * 2 + 2)
                    take_wait()
                    pool.indirect_dma_start(out=k.ybuf, out_offset=bass.IndirectOffsetOnAxis(ap=iy[:, p:p + 1], axis=0),
                                            in_=y[:, p, :], in_offset=None, bounds_check=last_y,
                                            oob_is_err=False).then_inc(stored[p], 16)

                gather(0, 0, 1)
                gather(1, 1, 2)

                def turn(e, p, it):
                    pool.wait_ge(turned, e + 1)
                    pool.wait_ge(gathered[p], it * 16 + 16)
                    take_wait()
                    gather(e + 2, p, it * 4 + 2 * p + 3)
                    wait(pool, stored[p], it * 16)
                    take_wait()
                    scatter(e, p, it * 4 + 2 * p + 4)

                for p in range(2):
                    turn(p, p, 0)
                with pool.Fori(1, NE // 2 - 1) as it:
                    for p in range(2):
                        turn(it * 2 + p, p, it)
                for p in range(2):
                    pool.wait_ge(stored[p], 16 * (NE // 2 - 1))
                    scatter(NE - 2 + p, p, 2 * NE - 1 + p)

                def over(j):
                    pool.wait_ge(o_index, j * 2 + 2)
                    take_wait()
                    pool.indirect_dma_start(out=xg[:, 0, :], out_offset=None, in_=k.hbuf,
                                            in_offset=bass.IndirectOffsetOnAxis(ap=ih[:, 0:1], axis=0),
                                            bounds_check=last_h, oob_is_err=False).then_inc(o_gathered, 16)
                    pool.wait_ge(o_y, j * 2 + 2)
                    take_wait()
                    pool.indirect_dma_start(out=k.ybuf, out_offset=bass.IndirectOffsetOnAxis(ap=over_slot[:, 0:1], axis=0),
                                            in_=y[:, 0, :], in_offset=None, bounds_check=last_y,
                                            oob_is_err=False).then_inc(o_stored, 16)
                turns_over(pool, over)

            @block.tensor
            def _(pe):
                TRN, GATE, UP, DOWN = 0, 2, 3, 4

                def turn_tokens(p, done):
                    for j in range(KD):
                        mm = pe.transpose(ps[:, TRN + j // 4, (j % 4) * P:(j % 4 + 1) * P], xg[:, p, j * P:(j + 1) * P], ident[:])
                    mm.then_inc(done, 1)

                def gate_up(p, done):
                    for f in range(2 * KF):
                        for j in range(KD):
                            mm = pe.matmul(ps[:, GATE + f // KF, (f % KF) * P:(f % KF + 1) * P], wgu[:, p, j, f * P:(f + 1) * P], xT[:, p, j, :],
                                           start=(j == 0), stop=(j == KD - 1))
                    mm.then_inc(done, 1)

                def down(p, done):
                    for half in range(2):
                        for j in range(KF):
                            mm = pe.matmul(ps[:, DOWN + half, :], hh[:, p, j, :], wd[:, p, j, 512 * half:512 * half + 512],
                                           start=(j == 0), stop=(j == KF - 1))
                    mm.then_inc(done, 1)

                pe.wait_ge(gathered[0], 16)
                turn_tokens(0, turned)
                pe.wait_ge(xT_ready, 2)
                pe.wait_ge(gu_loaded[0], 32)
                gate_up(0, gu_done)
                pe.wait_ge(gathered[1], 16)
                turn_tokens(1, turned)

                def down_of(e, p, n):
                    pe.wait_ge(hh_ready, e + 1)
                    pe.wait_ge(wd_loaded[p], n * 16 + 16)
                    down(p, d_done)

                def turn(e, p, it):
                    first = it + 1 if p == 0 else it
                    pe.wait_ge(xT_ready, e * 2 + 2)
                    pe.wait_ge(gu_loaded[p], first * 32 + 32)
                    pe.wait_ge(hh_ready, e)
                    gate_up(p, gu_done)
                    pe.wait_ge(gathered[1 - p], it * 16 + 32)
                    turn_tokens(1 - p, turned)
                    wait(pe, y_ready, e * 2 - 2)
                    down_of(e - 1, 1 - p, it)
                turns(pe, turn)
                e = NE - 1
                pe.wait_ge(xT_ready, 2 * e + 2)
                pe.wait_ge(gu_loaded[1], 32 * (NE // 2))
                pe.wait_ge(hh_ready, e)
                gate_up(1, gu_done)
                pe.wait_ge(y_ready, e * 2 - 2)
                down_of(e - 1, 0, NE // 2 - 1)
                pe.wait_ge(y_ready, e * 2)
                down_of(e, 1, NE // 2 - 1)

                def over(j):
                    pe.wait_ge(o_gathered, j * 16 + 16)
                    turn_tokens(0, o_turned)
                    pe.wait_ge(o_xT, j * 2 + 2)
                    pe.wait_ge(o_w, j * 32 + 32)
                    gate_up(0, o_gu)
                    pe.wait_ge(o_hh, j + 1)
                    down(0, o_d)
                turns_over(pe, over)

            @block.scalar
            def _(act):
                def silu(e, done, out):
                    act.wait_ge(done, e + 1)
                    act.activation(sg[:], ps[:, 2, :], ACT.Silu).then_inc(out, 1)

                def y_evacuate(p, out):
                    for half in range(2):
                        act.activation(y[:, p, 512 * half:512 * half + 512], ps[:, 4 + half, :], ACT.Copy).then_inc(out, 1)

                silu(0, gu_done, silu_ready)

                def turn(e, p, it):
                    act.wait_ge(hh_ready, e)
                    silu(e, gu_done, silu_ready)
                    act.wait_ge(d_done, e)
                    wait(act, stored[1 - p], it * 16)
                    y_evacuate(1 - p, y_ready)
                turns(act, turn)
                act.wait_ge(hh_ready, NE - 1)
                silu(NE - 1, gu_done, silu_ready)
                act.wait_ge(d_done, NE - 1)
                act.wait_ge(stored[0], 16 * (NE // 2 - 1))
                y_evacuate(0, y_ready)
                act.wait_ge(d_done, NE)
                act.wait_ge(stored[1], 16 * (NE // 2 - 1))
                y_evacuate(1, y_ready)

                def over(j):
                    silu(j, o_gu, o_silu)
                    act.wait_ge(o_d, j + 1)
                    y_evacuate(0, o_y)
                turns_over(act, over)

            @block.vector
            def _(dve):
                def xT_evacuate(p, out):
                    for half in range(2):
                        dve.tensor_tensor(xT[:, p, 4 * half:4 * half + 4, :], ps[:, half, :].rearrange("p (k t) -> p k t", k=4),
                                          g_moe[:, 4 * half:4 * half + 4].unsqueeze(2).to_broadcast([P, 4, P]), ALU.mult).then_inc(out, 1)

                def times_up(p, out):
                    dve.tensor_tensor(hh[:, p, :, :].rearrange("p k t -> p (k t)"), sg[:], ps[:, 3, :], ALU.mult).then_inc(out, 1)

                dve.wait_ge(turned, 1)
                xT_evacuate(0, xT_ready)
                dve.wait_ge(silu_ready, 1)
                times_up(0, hh_ready)
                dve.wait_ge(turned, 2)
                xT_evacuate(1, xT_ready)

                def turn(e, p, it):
                    dve.wait_ge(silu_ready, e + 1)
                    times_up(p, hh_ready)
                    dve.wait_ge(turned, e + 2)
                    xT_evacuate(1 - p, xT_ready)
                turns(dve, turn)
                dve.wait_ge(silu_ready, NE)
                times_up(1, hh_ready)

                def over(j):
                    dve.wait_ge(o_idx, j * 16 + 16)
                    dve.tensor_scalar(over_h[:], over_slot[:], float(T), float(-T), ALU.is_ge, ALU.mult).then_inc(o_index, 1)
                    dve.wait_ge(o_index, j * 2 + 1)
                    dve.tensor_tensor(ih[:, 0:1], over_slot[:], over_h[:], ALU.add).then_inc(o_index, 1)
                    dve.wait_ge(o_turned, j + 1)
                    xT_evacuate(0, o_xT)
                    dve.wait_ge(o_silu, j + 1)
                    times_up(0, o_hh)
                turns_over(dve, over)
                for i in range(NT):
                    dve.wait_ge(y_loaded[i], 32)
                    for j in range(2):
                        dve.scalar_tensor_tensor(out=x[:, i, :], in0=wgu[:, j, i, :], scalar=gates[:, j, i:i + 1], in1=x[:, i, :],
                                                 op0=ALU.mult, op1=ALU.add).then_inc(x_sum, 1)
                        if j == 0:
                            dve.wait_ge(x_sum, 2 * i + 1)


def conformer(k):
    nc, x, ident, mhalf, ps, I = k.nc, k.x, k.ident, k.mhalf, k.ps, k.i
    POOL_TAPS = 11
    DVE_TAPS = TAPS - POOL_TAPS
    CT = D // P
    with ExitStack() as outer:
        osb = lambda name, shape, dt=F32: outer.enter_context(nc.sbuf_tensor(name, shape, dt))
        osem = semaphores(nc, outer)
        w_pw2 = osb("w_pw2", [P, KD, D])
        conv = osb("conv", [P, CT, T])
        ln_g, ln_b = osb("ln_g", [P, CT]), osb("ln_b", [P, CT])
        pw2_loaded = osem("pw2_loaded")
        with ExitStack() as ctx:
            sb = lambda name, shape, dt=F32: ctx.enter_context(nc.sbuf_tensor(name, shape, dt))
            sem = semaphores(nc, ctx)
            hT = sb("c_hT", [P, KD, T])
            wa, wg = sb("wa", [P, 2, KD, P]), sb("wg", [P, 2, KD, P])
            g_c = sb("g_c", [P, KD])
            b_pw1 = sb("b_pw1", [P, 2 * CT])
            taps = sb("taps", [P, CT, TAPS])
            b_dw = sb("b_dw", [P, CT])
            small_loaded, squared, rstd_ready = sem("c_small"), sem("c_squared"), sem("c_rstd_ready")
            h_ready, turned, hT_ready, dve_link, pool_link = sem("c_h_ready"), sem("c_turned"), sem("c_hT_ready"), sem("c_dve_link"), sem("c_pool_link")
            biased = sem("biased")
            w_loaded = [sem("w_loaded0_"), sem("w_loaded1_")]

            def load_w(sp, c, p):
                w = I["conv_w_pw1"].rearrange("a (k p) n -> p (a k) n", p=P)
                sp.dma_start(wa[:, p, :, :], w[:, :, bass.ds(c * P, P)]).then_inc(w_loaded[p], 16)
                sp.dma_start(wg[:, p, :, :], w[:, :, bass.ds(c * P + D, P)]).then_inc(w_loaded[p], 16)

            with ExitStack() as c1:
                ss, rstd = (c1.enter_context(nc.sbuf_tensor(n, [P, NT], F32)) for n in ("c_ss", "c_rstd"))
                h = c1.enter_context(nc.sbuf_tensor("c_h", [P, 2, D], F32))
                sq = c1.enter_context(nc.sbuf_tensor("c_sq", [P, D], F32))
                b_pw2 = c1.enter_context(nc.sbuf_tensor("b_pw2", [P, D], F32))
                block = c1.enter_context(nc.Block())

                def turns(eng, turn):
                    with eng.Fori(0, NT // 2 - 1) as it:
                        for p in range(2):
                            turn(it * 2 + p, p, True)
                    for p in range(2):
                        turn(NT - 2 + p, p, False)

                @block.sync
                def _(sp):
                    col = lambda name: I[name].rearrange("a (k p) -> p (a k)", p=P)
                    with nc.allow_non_contiguous_dma(reason="per-channel vectors"):
                        for dst, src in ((g_c, col("conv_norm_g")), (b_pw1, col("conv_b_pw1")), (b_dw, col("conv_b_dw")),
                                         (ln_g, col("conv_ln_g")), (ln_b, col("conv_ln_b"))):
                            sp.dma_start(dst[:], src).then_inc(small_loaded, 16)
                        for c in range(CT):
                            sp.dma_start(taps[:, c, :], I["conv_w_dw"][0, :, c * P:(c + 1) * P].rearrange("j p -> p j")).then_inc(small_loaded, 16)
                    sp.dma_start(b_pw2[:], I["conv_b_pw2"][0, :].partition_broadcast(P)).then_inc(small_loaded, 16)
                    for p in range(2):
                        load_w(sp, p, p)
                    sp.dma_start(w_pw2[:, :, :], I["conv_w_pw2"].rearrange("a (k p) n -> p (a k) n", p=P)).then_inc(pw2_loaded, 16)

                @block.scalar
                def _(act):
                    for i in range(NT):
                        if i:
                            act.wait_ge(squared, i)
                        act.activation(sq[:], x[:, i, :], ACT.Square, accum_out=ss[:, i:i + 1]).then_inc(squared, 1)

                @block.gpsimd
                def _(pool):
                    link = Link(pool, pool_link)
                    pool.wait_ge(squared, NT)
                    link(pool.tensor_scalar(ss[:], ss[:], 1.0 / D, RMS_EPS, ALU.mult, ALU.add))
                    pool.tensor_tensor(rstd[:], ss[:], mhalf[:, 0:NT], ALU.pow).then_inc(rstd_ready, 1)
                    pool.wait_ge(small_loaded, 16 * 14)

                    def turn(i, p, more):
                        pool.wait_ge(h_ready, i + 1)
                        pool.tensor_tensor(x[:, at(i), :], x[:, at(i), :], b_pw2[:, :].unsqueeze(1), ALU.add).then_inc(biased, 1)
                    turns(pool, turn)

                @block.tensor
                def _(pe):
                    def turn(i, p, more):
                        pe.wait_ge(h_ready, i + 1)
                        for j in range(KD):
                            mm = pe.transpose(ps[:, 2 * p + j // 4, (j % 4) * P:(j % 4 + 1) * P], h[:, p, j * P:(j + 1) * P], ident[:])
                        mm.then_inc(turned, 1)
                    turns(pe, turn)

                @block.vector
                def _(dve):
                    def normalise(i, p):
                        dve.tensor_scalar(h[:, p:p + 1, :], x[:, at(i), :], rstd[:, at(i)], None, ALU.mult).then_inc(h_ready, 1)

                    dve.wait_ge(rstd_ready, 1)
                    normalise(0, 0)
                    normalise(1, 1)
                    dve.wait_ge(small_loaded, 16 * 14)

                    def turn(i, p, more):
                        dve.wait_ge(turned, i + 1)
                        for half in range(2):
                            dve.tensor_tensor(hT[:, 4 * half:4 * half + 4, bass.ds(i * P, P)], ps[:, 2 * p + half, :].rearrange("p (k t) -> p k t", k=4),
                                              g_c[:, 4 * half:4 * half + 4].unsqueeze(2).to_broadcast([P, 4, P]), ALU.mult).then_inc(hT_ready, 1)
                        if more:
                            normalise(i + 2, p)
                    turns(dve, turn)

            with ExitStack() as c2:
                sb2 = lambda name, shape: c2.enter_context(nc.sbuf_tensor(name, shape, F32))
                sem2 = semaphores(nc, c2)
                sig = sb2("sig", [P, 2, 512])
                u = sb2("u", [P, 2, HALO + T])
                wt = sb2("wt", [P, 2, TAPS])
                gate_bias = sb2("gate_bias", [P, 2])
                acc = sb2("acc", [P, 2, T])
                prod = sb2("prod", [P, 2, T])
                pacc = sb2("pacc", [P, T])
                proj, sig_ready, u_ready, wt_ready = sem2("proj"), sem2("sig_ready"), sem2("u_ready"), sem2("wt_ready")
                tapped, prod_ready, added, conv_ready = sem2("tapped"), sem2("prod_ready"), sem2("added"), sem2("conv_ready")
                zeroed, bias_ready = sem2("c_zeroed"), sem2("bias_ready")
                block = c2.enter_context(nc.Block())

                def tiles(eng, turn):
                    with eng.Fori(0, CT // 2) as it:
                        for p in range(2):
                            turn(it * 2 + p, p, it)

                @block.sync
                def _(sp):
                    with sp.Fori(0, CT // 2 - 1) as it:
                        for p in range(2):
                            sp.wait_ge(proj, it * 4 + 2 * p + 2)
                            load_w(sp, it * 2 + p + 2, p)

                @block.tensor
                def _(pe):
                    def turn(c, p, it):
                        pe.wait_ge(w_loaded[p], it * 32 + 32)
                        pe.wait_ge(u_ready, c * 2 + 2)
                        for half in range(2):
                            for bank, w in ((0, wa), (2, wg)):
                                for j in range(KD):
                                    mm = pe.matmul(ps[:, 4 * p + bank + half, :], w[:, p, j, :], hT[:, j, 512 * half:512 * half + 512],
                                                   start=(j == 0), stop=(j == KD - 1))
                            mm.then_inc(proj, 1)
                    tiles(pe, turn)

                @block.scalar
                def _(act):
                    def sigmoid(c, p, half):
                        act.wait_ge(proj, c * 2 + half + 1)
                        act.wait_ge(u_ready, c * 2 + half + 3)
                        act.activation(sig[:, half, :], ps[:, 4 * p + 2 + half, :], ACT.Sigmoid, bias=gate_bias[:, p:p + 1]).then_inc(sig_ready, 1)

                    def turn(c, p, it):
                        act.activation(gate_bias[:, p:p + 1], b_pw1[:, at(c + CT)], ACT.Copy).then_inc(bias_ready, 1)
                        act.wait_ge(bias_ready, c + 1)
                        for half in range(2):
                            sigmoid(c, p, half)
                        act.wait_ge(wt_ready, c + 1)
                        act.wait_ge(u_ready, c * 2 + 6)
                        act.wait_ge(conv_ready, c + 1)
                        for n in range(POOL_TAPS):
                            if n == 0:
                                act.activation(pacc[:], u[:, p, n:n + T], ACT.Copy, scale=wt[:, p, n:n + 1]).then_inc(prod_ready, 1)
                                continue
                            if n > 2:
                                act.wait_ge(added, c * (POOL_TAPS - 1) + n - 2)
                            act.activation(prod[:, n % 2, :], u[:, p, n:n + T], ACT.Copy, scale=wt[:, p, n:n + 1]).then_inc(prod_ready, 1)
                    tiles(act, turn)

                @block.gpsimd
                def _(pool):
                    pool.memset(u[:], 0.0).then_inc(zeroed, 1)

                    def turn(c, p, it):
                        for n in range(1, POOL_TAPS):
                            pool.wait_ge(prod_ready, c * POOL_TAPS + n + 1)
                            pool.tensor_tensor(pacc[:], pacc[:], prod[:, n % 2, :], ALU.add).then_inc(added, 1)
                            if n < POOL_TAPS - 1:
                                pool.wait_ge(added, c * (POOL_TAPS - 1) + n)
                    tiles(pool, turn)

                @block.vector
                def _(dve):
                    dve.wait_ge(zeroed, 1)
                    dve.sem_inc(u_ready, 4)
                    dve.sem_inc(conv_ready, 1)

                    def turn(c, p, it):
                        dve.tensor_copy(wt[:, p:p + 1, :], taps[:, at(c), :]).then_inc(wt_ready, 1)
                        for half in range(2):
                            dve.wait_ge(sig_ready, c * 2 + half + 1)
                            dve.scalar_tensor_tensor(out=u[:, p, HALO + 512 * half:HALO + 512 * half + 512], in0=ps[:, 4 * p + half, :],
                                                     scalar=b_pw1[:, at(c)], in1=sig[:, half, :], op0=ALU.add, op1=ALU.mult).then_inc(u_ready, 1)
                        dve.wait_ge(u_ready, c * 2 + 6)
                        dve.wait_ge(wt_ready, c + 1)
                        for n in range(DVE_TAPS):
                            j = POOL_TAPS + n
                            if n == 0:
                                ins = dve.tensor_scalar(acc[:, 0, :], u[:, p, j:j + T], wt[:, p, j:j + 1], b_dw[:, at(c)], ALU.mult, ALU.add)
                            elif n == 1:
                                ins = dve.tensor_scalar(acc[:, 1, :], u[:, p, j:j + T], wt[:, p, j:j + 1], None, ALU.mult)
                            else:
                                dve.wait_ge(tapped, c * (DVE_TAPS + 1) + n - 1)
                                ins = dve.scalar_tensor_tensor(out=acc[:, n % 2, :], in0=u[:, p, j:j + T], scalar=wt[:, p, j:j + 1], in1=acc[:, n % 2, :],
                                                               op0=ALU.mult, op1=ALU.add)
                            ins.then_inc(tapped, 1)
                        dve.wait_ge(tapped, c * (DVE_TAPS + 1) + DVE_TAPS)
                        dve.tensor_tensor(acc[:, 0, :], acc[:, 0, :], acc[:, 1, :], ALU.add).then_inc(tapped, 1)
                        dve.wait_ge(tapped, c * (DVE_TAPS + 1) + DVE_TAPS + 1)
                        dve.wait_ge(added, c * (POOL_TAPS - 1) + POOL_TAPS - 1)
                        dve.tensor_tensor(conv[:, at(c), :], acc[:, 0:1, :], pacc[:, :].unsqueeze(1), ALU.add).then_inc(conv_ready, 1)
                    tiles(dve, turn)

        with ExitStack() as ctx:
            sb = lambda name, shape, dt=F32: ctx.enter_context(nc.sbuf_tensor(name, shape, dt))
            sem = semaphores(nc, ctx)
            cs = sb("cs", [P, 2, CT, P])
            stats = sb("stats", [P, 2, 6])
            mv = sb("mv", [P, 2])
            rs = sb("rs", [P, 1])
            nb = sb("nb", [P, 1])
            un = sb("un", [P, D])
            yT = sb("c_yT", [P, 2, CT, P])
            dve_waited, waited = sem("c_dve_waited"), sem("c_waited")
            staged, turned1, stats_ready, mv_ready, eps_ready, rs_ready, nb_ready = (sem(n) for n in (
                "staged", "turned1", "stats_ready", "mv_ready", "eps_ready", "rs_ready", "nb_ready"))
            un_ready, turned2, yT_ready, pw2_done, x_added = (sem(n) for n in ("un_ready", "turned2", "c_yT_ready", "pw2_done", "c_x_added"))
            block = ctx.enter_context(nc.Block())

            def turns(eng, turn):
                with eng.Fori(0, NT // 2 - 1) as it:
                    for p in range(2):
                        turn(it * 2 + p, p, True)
                turn(NT - 2, 0, True)
                turn(NT - 1, 1, False)

            @block.gpsimd
            def _(pool):
                def stage(i, p):
                    pool.tensor_copy(cs[:, p, :, :], conv[:, :, bass.ds(i * P, P)]).then_inc(staged, 1)

                def root(i):
                    pool.wait_ge(eps_ready, i + 1)
                    pool.tensor_tensor(rs[:], mv[:, 1:2], mhalf[:, 0:1], ALU.pow).then_inc(rs_ready, 1)

                stage(0, 0)
                stage(1, 1)
                root(0)

                def turn(i, p, more):
                    if more:
                        pool.wait_ge(rs_ready, i + 1)
                        pool.sem_inc(waited, 1)
                        if not isinstance(i, int) or i + 2 < NT:
                            stage(i + 2, p)
                        root(i + 1)
                turns(pool, turn)

            @block.tensor
            def _(pe):
                pe.wait_ge(pw2_loaded, 16)

                def turn_conv(i, p):
                    pe.wait_ge(staged, i + 1)
                    for j in range(CT):
                        mm = pe.transpose(ps[:, j // 4, (j % 4) * P:(j % 4 + 1) * P], cs[:, p, j, :], ident[:])
                    mm.then_inc(turned1, 1)

                def turn_back(i):
                    pe.wait_ge(un_ready, i * 2 + 2)
                    for j in range(CT):
                        mm = pe.transpose(ps[:, 2 + j // 4, (j % 4) * P:(j % 4 + 1) * P], un[:, j * P:(j + 1) * P], ident[:])
                    mm.then_inc(turned2, 1)

                def project(i, p, half):
                    for j in range(CT):
                        mm = pe.matmul(ps[:, 4 + 2 * p + half, :], yT[:, p, j, :], w_pw2[:, j, 512 * half:512 * half + 512], start=(j == 0), stop=(j == CT - 1))
                    mm.then_inc(pw2_done, 1)

                turn_conv(0, 0)
                turn_back(0)

                def turn(i, p, more):
                    if more:
                        pe.wait_ge(un_ready, i * 2 + 2)
                        turn_conv(i + 1, 1 - p)
                    pe.wait_ge(yT_ready, i * CT + CT)
                    pe.wait_ge(x_added, i * 2 + 2)
                    project(i, p, 0)
                    if more:
                        turn_back(i + 1)
                    project(i, p, 1)
                turns(pe, turn)

            @block.scalar
            def _(act):
                def normalise(i):
                    act.wait_ge(nb_ready, i + 1)
                    for half in range(2):
                        act.activation(un[:, 512 * half:512 * half + 512], ps[:, half, :], ACT.Identity, bias=nb[:, 0:1], scale=rs[:, 0:1]).then_inc(un_ready, 1)

                def silu(i, p):
                    act.wait_ge(turned2, i + 1)
                    for j in range(CT):
                        act.activation(yT[:, p, j, :], ps[:, 2 + j // 4, (j % 4) * P:(j % 4 + 1) * P], ACT.Silu,
                                       bias=ln_b[:, j:j + 1], scale=ln_g[:, j:j + 1]).then_inc(yT_ready, 1)

                normalise(0)
                silu(0, 0)

                def turn(i, p, more):
                    if more:
                        act.wait_ge(turned2, i + 1)
                        normalise(i + 1)
                        silu(i + 1, 1 - p)
                turns(act, turn)

            @block.vector
            def _(dve):
                dve.sem_inc(x_added, 4)

                def statistics(i):
                    dve.wait_ge(turned1, i + 1)
                    for half in range(2):
                        dve.bn_stats(stats[:, half, :], ps[:, half, :]).then_inc(stats_ready, 1)
                    dve.wait_ge(stats_ready, i * 2 + 2)
                    dve.sem_inc(dve_waited, 1)
                    dve.bn_aggr(mv[:], stats[:]).then_inc(mv_ready, 1)
                    dve.wait_ge(mv_ready, i + 1)
                    dve.tensor_scalar(mv[:, 1:2], mv[:, 1:2], LN_EPS, None, ALU.add).then_inc(eps_ready, 1)
                    dve.wait_ge(rs_ready, i + 1)
                    dve.scalar_tensor_tensor(out=nb[:], in0=mv[:, 0:1], scalar=-1.0, in1=rs[:], op0=ALU.mult, op1=ALU.mult).then_inc(nb_ready, 1)

                statistics(0)

                def turn(i, p, more):
                    if more:
                        statistics(i + 1)
                    for half in range(2):
                        dve.wait_ge(pw2_done, i * 2 + half + 1)
                        dve.tensor_tensor(x[:, at(i), 512 * half:512 * half + 512], ps[:, 4 + 2 * p + half:5 + 2 * p + half, :],
                                          x[:, at(i), 512 * half:512 * half + 512], ALU.add).then_inc(x_added, 1)
                turns(dve, turn)


INPUTS = ["x", "mix_norm_g", "w_in", "q_norm_g", "k_norm_g", "attn_sinks", "ssm_conv_w", "ssm_conv_b",
          "ssm_dt_bias", "ssm_a_log", "ssm_d", "ssm_out_norm_g", "w_out", "conv_norm_g", "conv_w_pw1",
          "conv_b_pw1", "conv_w_dw", "conv_b_dw", "conv_ln_g", "conv_ln_b", "conv_w_pw2", "conv_b_pw2",
          "moe_norm_g", "moe_w_group", "moe_b_group", "moe_w_expert", "moe_b_expert", "moe_w_gate_up",
          "moe_w_down"]


def kernel(**inputs):
    import concourse.bacc as bacc
    from concourse.bass_utils import run_bass_kernel_spmd

    nc = bacc.Bacc("TRN2", target_bir_lowering=False, num_devices=1)
    arrays, aps = {}, {}
    for name in INPUTS:
        a = np.ascontiguousarray(inputs[name])
        arrays[f"in_{name}"] = a
        aps[name] = nc.dram_tensor(f"in_{name}", a.shape, mybir.dt.from_np(a.dtype), kind="ExternalInput").ap()
    out = nc.dram_tensor("out", (1, T, D), F32, kind="ExternalOutput").ap()
    Trunk(nc, aps, out).build()
    r = run_bass_kernel_spmd(nc, [arrays], core_ids=[0])
    return r.results[0]["out"]
```
